# Optimizing a Trainium2 kernel written in Bass

```python
import math
import jax, jax.numpy as jnp
from jax import lax
import numpy as np

D_MODEL = 1024
BATCH = 1
SEQ = 256
DEPTH = 2

N_MIXERS = 2
ATT_HEADS = 16
ATT_HEAD_DIM = D_MODEL // ATT_HEADS
MOBA_BLOCK = 256
MOBA_TOPK = 3
MOBA_Q_CHUNK = 64
RET_HEADS = 4
RET_KEY_DIM = D_MODEL // RET_HEADS
RET_VAL_DIM = 2 * RET_KEY_DIM
RET_CHUNK = 128
FFN_DIM = 2816
CONV_WIDTH = 3
LN_EPS = 1e-5
GN_EPS = 1e-5
DEEPNORM_ALPHA = (2.0 * DEPTH) ** 0.25
DEEPNORM_BETA = (8.0 * DEPTH) ** -0.25
N_ATT_LAYERS = (DEPTH + 1) // 2
N_RET_LAYERS = DEPTH // 2
NEG_INF = -1e30

kernel_name = "moba_retnet_interleaved_deepnorm_convffn"

def layer_norm(x, g, b):
    xf = x.astype(jnp.float32)
    mu = jnp.mean(xf, axis=-1, keepdims=True)
    var = jnp.mean(jnp.square(xf - mu), axis=-1, keepdims=True)
    y = (xf - mu) * lax.rsqrt(var + LN_EPS)
    return (y * g + b).astype(x.dtype)

def moba_attention(x, w_in, w_out):
    B, S, _ = x.shape
    H, hd = ATT_HEADS, ATT_HEAD_DIM
    QC, BLK = MOBA_Q_CHUNK, MOBA_BLOCK
    q, k, v = jnp.split(x @ w_in, 3, axis=-1)

    def heads(t):
        return t.reshape(B, S, H, hd).transpose(0, 2, 1, 3)

    q = heads(q) * (hd ** -0.5)
    k, v = heads(k), heads(v)
    n_blk = -(-S // BLK)
    s_pad = n_blk * BLK
    pad = ((0, 0), (0, 0), (0, s_pad - S), (0, 0))
    k_blk = jnp.pad(k, pad).reshape(B, H, n_blk, BLK, hd)
    v_blk = jnp.pad(v, pad).reshape(B, H, n_blk, BLK, hd)
    k_mean = jnp.mean(k_blk.astype(jnp.float32), axis=3).astype(k.dtype)
    n_q = S // QC
    q_chunks = q.reshape(B, H, n_q, QC, hd)
    top_k = min(MOBA_TOPK, n_blk)
    slopes = jnp.exp2(-8.0 * jnp.arange(1, H + 1, dtype=jnp.float32) / H)
    h_idx = jnp.arange(H)[:, None, None]
    blk_ids = jnp.arange(n_blk)
    offs = jnp.arange(BLK)

    def one_chunk(n):
        b = n // n_q
        c = n % n_q
        qc = q_chunks[b, :, c]
        t = c * QC + jnp.arange(QC)
        j = (c * QC) // BLK
        kb, vb, km = k_blk[b], v_blk[b], k_mean[b]
        gate = jnp.einsum('hqd,hnd->hqn', qc, km).astype(jnp.float32)
        gate = jnp.where(blk_ids < j, gate, NEG_INF)
        _, sel = lax.top_k(gate, top_k)
        sel_ok = jnp.arange(top_k) < j
        sel = jnp.where(sel_ok, sel, 0)
        k_sel = kb[h_idx, sel]
        v_sel = vb[h_idx, sel]
        s_sel = jnp.einsum('hqd,hqrkd->hqrk', qc, k_sel).astype(jnp.float32)
        pos_sel = sel[..., None] * BLK + offs
        dist_sel = (t[None, :, None, None] - pos_sel).astype(jnp.float32)
        s_sel = s_sel - slopes[:, None, None, None] * dist_sel
        s_sel = jnp.where(sel_ok[None, None, :, None], s_sel, NEG_INF)
        s_sel = s_sel.reshape(H, QC, top_k * BLK)
        k_own = lax.dynamic_index_in_dim(kb, j, axis=1, keepdims=False)
        v_own = lax.dynamic_index_in_dim(vb, j, axis=1, keepdims=False)
        dist_own = (t[:, None] - (j * BLK + offs)[None, :]).astype(jnp.float32)
        s_own = jnp.einsum('hqd,hkd->hqk', qc, k_own).astype(jnp.float32)
        s_own = s_own - slopes[:, None, None] * dist_own
        s_own = jnp.where(dist_own >= 0, s_own, NEG_INF)
        p = jax.nn.softmax(jnp.concatenate([s_sel, s_own], axis=-1), axis=-1).astype(v.dtype)
        p_sel = p[..., :top_k * BLK].reshape(H, QC, top_k, BLK)
        p_own = p[..., top_k * BLK:]
        return (jnp.einsum('hqrk,hqrkd->hqd', p_sel, v_sel)
                + jnp.einsum('hqk,hkd->hqd', p_own, v_own))

    out = lax.map(one_chunk, jnp.arange(B * n_q))
    out = out.reshape(B, n_q, H, QC, hd).transpose(0, 1, 3, 2, 4).reshape(B, S, H * hd)
    return out @ w_out

def retention(x, w_in, w_out, gn_g, gn_b):
    B, S, _ = x.shape
    H, dk, dv, C = RET_HEADS, RET_KEY_DIM, RET_VAL_DIM, RET_CHUNK
    q, k, v, g = jnp.split(x @ w_in, [H * dk, 2 * H * dk, 2 * H * dk + H * dv], axis=-1)
    n_c = S // C

    def chunks(t, d):
        return t.reshape(B, n_c, C, H, d).transpose(1, 0, 3, 2, 4).astype(jnp.float32)

    qc = chunks(q, dk)
    kc = chunks(k, dk) * (dk ** -0.5)
    vc = chunks(v, dv)
    log_gamma = jnp.log1p(-jnp.exp2(-5.0 - jnp.arange(H, dtype=jnp.float32)))
    i = jnp.arange(C, dtype=jnp.float32)
    diff = i[:, None] - i[None, :]
    decay_in = jnp.where(diff >= 0, jnp.exp(log_gamma[:, None, None] * jnp.maximum(diff, 0.0)), 0.0)
    q_decay = jnp.exp(log_gamma[:, None] * (i + 1.0))
    k_decay = jnp.exp(log_gamma[:, None] * (C - 1.0 - i))
    chunk_decay = jnp.exp(log_gamma * C)

    def step(state, inp):
        qi, ki, vi = inp
        scores = jnp.einsum('bhqd,bhkd->bhqk', qi, ki) * decay_in
        inner = jnp.einsum('bhqk,bhkv->bhqv', scores, vi)
        cross = jnp.einsum('bhqd,bhdv->bhqv', qi * q_decay[..., None], state)
        state = (chunk_decay[:, None, None] * state
                 + jnp.einsum('bhkd,bhkv->bhdv', ki * k_decay[..., None], vi))
        return state, inner + cross

    state0 = jnp.zeros((B, H, dk, dv), jnp.float32)
    _, o = lax.scan(step, state0, (qc, kc, vc))
    o = o.transpose(1, 0, 3, 2, 4).reshape(B, S, H, dv)
    mu = jnp.mean(o, axis=-1, keepdims=True)
    var = jnp.mean(jnp.square(o - mu), axis=-1, keepdims=True)
    o = ((o - mu) * lax.rsqrt(var + GN_EPS)).reshape(B, S, H * dv)
    o = (o * gn_g + gn_b).astype(x.dtype) * jax.nn.silu(g)
    return o @ w_out

def conv_ffn(x, w_up, conv_w, conv_b, w_down):
    S = x.shape[1]
    u = x @ w_up
    u_pad = jnp.pad(u, ((0, 0), (CONV_WIDTH - 1, 0), (0, 0)))
    h = conv_b + conv_w[CONV_WIDTH - 1] * u_pad[:, CONV_WIDTH - 1:CONV_WIDTH - 1 + S]
    for w in range(CONV_WIDTH - 1):
        h = h + conv_w[w] * u_pad[:, w:w + S]
    a, gate = jnp.split(h, 2, axis=-1)
    return (jax.nn.gelu(a, approximate=False) * gate) @ w_down

def setup_inputs(seed: int = 0) -> dict:
    key = jax.random.key(seed)
    ks = jax.random.split(key, 16)
    f32 = jnp.float32
    D, F = D_MODEL, FFN_DIM
    ret_in = 2 * RET_HEADS * RET_KEY_DIM + 2 * RET_HEADS * RET_VAL_DIM
    ret_v = RET_HEADS * RET_VAL_DIM

    def nrm(k, shape, fan_in, scale=1.0):
        return jax.random.normal(k, shape, f32) * (fan_in ** -0.5) * scale

    return {
        "x": jax.random.normal(ks[0], (BATCH, SEQ, D), f32),
        "att_w_in": nrm(ks[1], (N_ATT_LAYERS, D, 3 * D), D),
        "att_w_out": nrm(ks[2], (N_ATT_LAYERS, D, D), D, DEEPNORM_BETA),
        "ret_w_in": nrm(ks[3], (N_RET_LAYERS, D, ret_in), D),
        "ret_w_out": nrm(ks[4], (N_RET_LAYERS, ret_v, D), ret_v, DEEPNORM_BETA),
        "ret_gn_g": 1.0 + 0.02 * jax.random.normal(ks[5], (N_RET_LAYERS, ret_v), f32),
        "ret_gn_b": 0.02 * jax.random.normal(ks[6], (N_RET_LAYERS, ret_v), f32),
        "mix_ln_g": 1.0 + 0.02 * jax.random.normal(ks[7], (DEPTH, D), f32),
        "mix_ln_b": 0.02 * jax.random.normal(ks[8], (DEPTH, D), f32),
        "ffn_ln_g": 1.0 + 0.02 * jax.random.normal(ks[9], (DEPTH, D), f32),
        "ffn_ln_b": 0.02 * jax.random.normal(ks[10], (DEPTH, D), f32),
        "ffn_w_up": nrm(ks[11], (DEPTH, D, 2 * F), D),
        "ffn_conv_w": nrm(ks[12], (DEPTH, CONV_WIDTH, 2 * F), CONV_WIDTH),
        "ffn_conv_b": 0.02 * jax.random.normal(ks[13], (DEPTH, 2 * F), f32),
        "ffn_w_down": nrm(ks[14], (DEPTH, F, D), F, DEEPNORM_BETA),
    }

def reference(x, att_w_in, att_w_out, ret_w_in, ret_w_out, ret_gn_g, ret_gn_b,
              mix_ln_g, mix_ln_b, ffn_ln_g, ffn_ln_b, ffn_w_up, ffn_conv_w,
              ffn_conv_b, ffn_w_down):
    for i in range(DEPTH):
        slot = i // N_MIXERS
        if i % N_MIXERS == 0:
            y = moba_attention(x, att_w_in[slot], att_w_out[slot])
        else:
            y = retention(x, ret_w_in[slot], ret_w_out[slot], ret_gn_g[slot], ret_gn_b[slot])
        x = layer_norm(DEEPNORM_ALPHA * x + y, mix_ln_g[i], mix_ln_b[i])
        f = conv_ffn(x, ffn_w_up[i], ffn_conv_w[i], ffn_conv_b[i], ffn_w_down[i])
        x = layer_norm(DEEPNORM_ALPHA * x + f, ffn_ln_g[i], ffn_ln_b[i])
    return x


_drawn_inputs = setup_inputs


def setup_inputs(seed=0):
    import zlib

    import numpy as np

    out = dict(_drawn_inputs(seed))
    spreads = {}
    factors = {'ret_gn_g': 8.0, 'ret_gn_b': 8.0, 'ffn_conv_b': 5.871}
    for name, (base, spread) in spreads.items():
        noise = np.random.default_rng([zlib.crc32(name.encode()), seed]).standard_normal(out[name].shape)
        drawn = base * np.exp(spread * noise) if base else spread * noise
        out[name] = __import__('jax').numpy.asarray(drawn.astype(out[name].dtype))
    for name, factor in factors.items():
        out[name] = (out[name] * factor).astype(out[name].dtype)
    return out
```

```python
from contextlib import ExitStack

import concourse.bass as bass
from concourse import mybir

F32 = mybir.dt.float32
F32R = mybir.dt.float32r
ALU = mybir.AluOpType
ACT = mybir.ActivationFunctionType
AX_X = mybir.AxisListType.X

P = 128
SEQ = 256
TT = SEQ // P
D = 1024
KD = D // P
HEADS = 16
HD = D // HEADS
QUADS = 4
RH = 4
RK = D // RH
RV = 2 * RK
FFN = 2816
FT = 2 * FFN // P
PAIRS = FFN // 256
UNIT = 2048
RING = 3
HALF = 256
BANK = 512
LN_EPS = 1e-5
GN_EPS = 1e-5
ALPHA = (2.0 * 2) ** 0.25
MASKED = -1e33
CAUSAL = P + SEQ

U_ATT = 0
U_ATT_OUT = U_ATT + 3 * QUADS
U_FFN = [U_ATT_OUT + 4, 0]
U_RET = U_FFN[0] + 3 * PAIRS
U_RET_OUT = U_RET + 6 * RH
U_FFN[1] = U_RET_OUT + 8
UNITS = U_FFN[1] + 3 * PAIRS
LAST_UNIT = [U_FFN[0] - 1, U_RET - 1, U_FFN[1] - 1, UNITS - 1]

ACC_ATT, TR_ATT = [[0, 1], [2, 4]], [[5, 6], [7, 3]]
ACC_FFN, TR_FFN = [[0, 1], [2, 3]], [[6, 7], [4, 5]]
ACC_RET, TR_RET = [[1, 6], [4, 5]], [[2, 3], [0, 7]]
TR_IN = [[0, 1], [2, 3]]


def decoder_trunk(nc, x, att_w_in, att_w_out, ret_w_in, ret_w_out, ret_gn_g, ret_gn_b, mix_ln_g,
                  mix_ln_b, ffn_ln_g, ffn_ln_b, ffn_w_up, ffn_conv_w, ffn_conv_b, ffn_w_down, out):
    with ExitStack() as ctx:
        def sb(name, shape, dt=F32):
            return ctx.enter_context(nc.sbuf_tensor(name, shape, dt))

        def sem(name):
            return ctx.enter_context(nc.semaphore(name))

        raw = sb("raw", [P, RING, UNIT])
        whi = sb("whi", [P, RING, UNIT], F32R)
        wlo = sb("wlo", [P, RING, UNIT], F32R)
        xtok = sb("xtok", [P, TT, D])
        xh = sb("xh", [P, KD, SEQ], F32R)
        xl = sb("xl", [P, KD, SEQ], F32R)
        oh = sb("oh", [P, 2 * KD, SEQ], F32R)
        ol = sb("ol", [P, 2 * KD, SEQ], F32R)
        lnp = sb("lnp", [P, 2, 2, D])
        stage = sb("stage", [FT, 8, P])
        gstage = sb("gstage", [2 * KD, 2, P])
        par = sb("par", [P, 8 * FT + 2 * 2 * KD])
        ident = sb("ident", [P, P])
        dist = sb("dist", [P, CAUSAL])
        slopes = sb("slopes", [P, HEADS])
        decay = sb("decay", [P, RH, CAUSAL])
        powers = sb("powers", [P, 32])
        gbase = sb("gbase", [P, 32])
        gpow = sb("gpow", [P, 32])
        gkey = sb("gkey", [P, 2])
        nkey = sb("nkey", [P, 1])
        mhalf = sb("mhalf", [P, TT])
        gm = sb("gm", [P, 5, TT])
        gmean = sb("gmean", [P, TT])
        st6 = sb("st6", [P, TT, 2, 6])
        mv = sb("mv", [P, TT, 2])
        veps = sb("veps", [P, TT])
        rstd = sb("rstd", [P, TT])
        qT = sb("qT", [P, 2, SEQ])
        kT = sb("kT", [P, 2, SEQ])
        vt = sb("vt", [P, TT, BANK])
        sc = sb("sc", [P, 2, CAUSAL])
        pt = sb("pt", [P, 2, CAUSAL])
        nmax = sb("nmax", [P, 4, TT])
        rsum = sb("rsum", [P, 4, TT])
        rinv = sb("rinv", [P, 4, TT])
        ua = sb("ua", [P, 2, SEQ])
        ug = sb("ug", [P, 2, SEQ])
        ga = sb("ga", [P, 2, SEQ])
        zf = sb("zf", [P, 2, SEQ])
        zh = sb("zh", [P, 2, 2, SEQ], F32R)
        zl = sb("zl", [P, 2, 2, SEQ], F32R)
        onrm = sb("onrm", [P, TT, RV])
        ygn = sb("ygn", [P, 4, SEQ])
        sg = sb("sg", [P, 4, SEQ])
        ps = ctx.enter_context(nc.psum_tensor("ps", [P, 8, BANK], F32))

        x_loaded = sem("x_loaded")
        par_loaded = sem("par_loaded")
        lnp_loaded = [sem(f"lnp_loaded{i}") for i in range(4)]
        loaded = [sem(f"loaded{i}") for i in range(RING)]
        hi_done = sem("hi_done")
        lo_done = sem("lo_done")
        used = sem("used")
        stored = sem("stored")
        const_step = sem("const_step")
        par_turned = sem("par_turned")
        par_copied = sem("par_copied")
        acc_ready = sem("acc_ready")
        dve_ln = sem("dve_ln")
        var_ready = sem("var_ready")
        rstd_ready = sem("rstd_ready")
        x_ready = sem("x_ready")
        xt_turned = sem("xt_turned")
        xh_ready = sem("xh_ready")
        xl_ready = sem("xl_ready")
        q_copied = sem("q_copied")
        k_copied = sem("k_copied")
        v_copied = sem("v_copied")
        s_ready = sem("s_ready")
        biased = sem("biased")
        max_ready = sem("max_ready")
        exp_ready = sem("exp_ready")
        inv_ready = sem("inv_ready")
        p_ready = sem("p_ready")
        p_turned = sem("p_turned")
        pt_ready = sem("pt_ready")
        pv_done = sem("pv_done")
        o_hi = sem("o_hi")
        o_lo = sem("o_lo")
        rq_copied = sem("rq_copied")
        rk_copied = sem("rk_copied")
        rv_copied = [sem(f"rv_copied{m}") for m in range(TT)]
        rs_ready = sem("rs_ready")
        decayed = sem("decayed")
        ro_ready = sem("ro_ready")
        dve_gn = sem("dve_gn")
        gvar_ready = sem("gvar_ready")
        grstd_ready = sem("grstd_ready")
        on_ready = sem("on_ready")
        on_turned = sem("on_turned")
        y_ready = sem("y_ready")
        silu_done = sem("silu_done")
        gated = sem("gated")
        ro_hi = sem("ro_hi")
        ro_lo = sem("ro_lo")
        ffn = [{n: sem(f"{n}_{l}") for n in (
            "scaled", "tap1", "taps_done", "gelu_done", "mult_done", "zh_done", "z_ready")}
            for l in range(2)]

        def cols(t, slot):
            return t[:, slot].rearrange("p (k n) -> p k n", k=KD)

        def rows(t, slot):
            return t[:, slot].rearrange("p (k n) -> p k n", k=2)

        def quarter(t, slot):
            return t[:, slot].rearrange("p (k n) -> p k n", k=4)

        def halves(bank):
            return ps[:, bank, :].rearrange("p (j n) -> p j n", j=2)

        def up_bank(part, s):
            return ps[:, 4 + 2 * part + s, 0:SEQ]

        def tap(l, w):
            return (4 * l + w) * FT

        def up_unit(l, i, part):
            return U_FFN[l] + part if isinstance(i, int) and i == 0 else U_FFN[l] - 1 + part

        def score_bank(t, h):
            return 3 if isinstance(t, int) and t == QUADS - 1 else 3 + h % 2

        GN = 8 * FT

        def load(sp, c, i, view, src):
            s = c % RING
            if not (isinstance(i, int) and c + RING * i < RING):
                sp.wait_ge(lo_done, c + RING * i - RING + 1)
            sp.dma_start(view(raw, s), src).then_inc(loaded[s], 16)

        def split_hi(act, c, i=0):
            if isinstance(i, int) and c + RING * i >= UNITS:
                return
            s = c % RING
            act.wait_ge(loaded[s], 16 * (c // RING + i + 1))
            if not (isinstance(i, int) and c + RING * i < RING):
                act.wait_ge(used, c + RING * i - RING + 1)
            nc.scalar.activation(whi[:, s], raw[:, s], ACT.Copy).then_inc(hi_done, 1)

        def split_lo(dve, c, i=0):
            if isinstance(i, int) and c + RING * i >= UNITS:
                return
            s = c % RING
            dve.wait_ge(hi_done, c + RING * i + 1)
            nc.vector.tensor_tensor(wlo[:, s], raw[:, s], whi[:, s].bitcast(F32),
                                    ALU.subtract).then_inc(lo_done, 1)

        def products(dst, ah, al, bh, bl, start, stop):
            nc.tensor.matmul(dst, ah, bh, start=start, stop=False)
            nc.tensor.matmul(dst, ah, bl, start=False, stop=False)
            return nc.tensor.matmul(dst, al, bh, start=False, stop=stop)

        def unit_ready(pe, c, i=0):
            pe.wait_ge(lo_done, c + RING * i + 1)

        def feature_tile(dst, c, j, ks=range(KD)):
            h, l = cols(whi, c % RING), cols(wlo, c % RING)
            for k in ks:
                last = products(dst, h[:, k, j * P:(j + 1) * P], l[:, k, j * P:(j + 1) * P],
                                xh[:, k, :], xl[:, k, :], k == 0, k == KD - 1)
            return last

        def out_rows(acc, ah, al, c, m, kk, first, last):
            h, l = rows(whi, c % RING), rows(wlo, c % RING)
            for n in range(2):
                b = slice(n * BANK, (n + 1) * BANK)
                ins = products(ps[:, acc[m][n], :], ah[:, m * P:(m + 1) * P], al[:, m * P:(m + 1) * P],
                               h[:, kk, b], l[:, kk, b], first, last)
            return ins

        consts = {}

        block = ctx.enter_context(nc.Block())

        @block.sync
        def _(sp):
            def in_cols(w, at):
                return w[:, bass.ds(at, 256)].rearrange("(k p) n -> p k n", p=P)

            def in_rows(w, at):
                return w[bass.ds(at, 256), :].rearrange("(k p) n -> p k n", p=P)

            def ln_params(slot, n, g, b):
                for i, v in enumerate((g, b)):
                    sp.dma_start(lnp[:, slot, i, :], v.partition_broadcast(P)).then_inc(lnp_loaded[n], 16)

            sp.dma_start(xtok[:, :, :], x[0].rearrange("(m p) d -> p m d", p=P)).then_inc(x_loaded, 16)

            for j in range(3):
                load(sp, j, 0, cols, in_cols(att_w_in[0], j * D))
            for l in range(2):
                sp.dma_start(stage[:, 4 * l:4 * l + 3, :],
                             ffn_conv_w[l].rearrange("w (f p) -> f w p", p=P)).then_inc(par_loaded, 16)
                sp.dma_start(stage[:, 4 * l + 3, :],
                             ffn_conv_b[l].rearrange("(f p) -> f p", p=P)).then_inc(par_loaded, 16)
            for i, v in enumerate((ret_gn_g, ret_gn_b)):
                sp.dma_start(gstage[:, i, :], v[0].rearrange("(f p) -> f p", p=P)).then_inc(par_loaded, 16)
            with sp.Fori(1, QUADS) as t:
                for j in range(3):
                    load(sp, j, t, cols, in_cols(att_w_in[0], t * 256 + j * D))
            ln_params(0, 0, mix_ln_g[0], mix_ln_b[0])
            for j in range(4):
                load(sp, U_ATT_OUT + j, 0, rows, in_rows(att_w_out[0], j * 256))
            ln_params(1, 1, ffn_ln_g[0], ffn_ln_b[0])

            def ffn_loads(l):
                u = U_FFN[l]
                load(sp, u, 0, cols, in_cols(ffn_w_up[l], 0))
                load(sp, u + 1, 0, cols, in_cols(ffn_w_up[l], FFN))
                with sp.Fori(1, PAIRS) as i:
                    load(sp, u - 1, i, cols, in_cols(ffn_w_up[l], i * 256))
                    load(sp, u, i, cols, in_cols(ffn_w_up[l], i * 256 + FFN))
                    load(sp, u + 1, i, rows, in_rows(ffn_w_down[l], i * 256 - 256))
                load(sp, u + 3 * PAIRS - 1, 0, rows, in_rows(ffn_w_down[l], FFN - 256))

            ffn_loads(0)
            sp.wait_ge(x_ready, TT)
            ln_params(0, 2, mix_ln_g[1], mix_ln_b[1])
            with sp.Fori(0, RH) as h:
                for j in range(2):
                    load(sp, U_RET + j, 2 * h, cols, in_cols(ret_w_in[0], h * RK + j * D))
                for j in range(2):
                    load(sp, U_RET + 2 + j, 2 * h, quarter,
                         ret_w_in[0][j * BANK:(j + 1) * BANK, bass.ds(h * RV + 2 * D, RV)]
                         .rearrange("(k p) n -> p k n", p=P))
                for j in range(2):
                    load(sp, U_RET + 4 + j, 2 * h, cols, in_cols(ret_w_in[0], h * RV + 4 * D + j * 256))
            for j in range(8):
                load(sp, U_RET_OUT + j, 0, rows, in_rows(ret_w_out[0], j * 256))
            sp.wait_ge(x_ready, 2 * TT)
            ln_params(1, 3, ffn_ln_g[1], ffn_ln_b[1])
            ffn_loads(1)
            for m in range(TT):
                sp.wait_ge(x_ready, 3 * TT + m + 1)
                sp.dma_start(out[0, m * P:(m + 1) * P, :], xtok[:, m, :]).then_inc(stored, 16)
            sp.wait_ge(stored, 16 * TT)

        @block.gpsimd
        def _(pool):
            n = [0]

            def step(ins):
                n[0] += 1
                ins.then_inc(const_step, 1)
                pool.wait_ge(const_step, n[0])

            step(nc.gpsimd.memset(ident[:], 0.0))
            step(nc.gpsimd.affine_select(out=ident[:], in_=ident[:], compare_op=ALU.not_equal, fill=1.0,
                                         base=0, pattern=[[-1, P]], channel_multiplier=1))
            for m, (a, b) in enumerate(((0, P), (P, CAUSAL))):
                step(nc.gpsimd.iota(dist[:, a:b], pattern=[[1, b - a]], base=-m * P, channel_multiplier=-1,
                                    allow_small_or_imprecise_dtypes=True))
                step(nc.gpsimd.affine_select(out=dist[:, a:b], in_=dist[:, a:b], compare_op=ALU.is_ge,
                                             fill=MASKED, base=m * P, pattern=[[-1, b - a]],
                                             channel_multiplier=1))
            for h in range(HEADS):
                nc.gpsimd.memset(slopes[:, h:h + 1], 2.0 ** (-8.0 * (h + 1) / HEADS))
            step(nc.gpsimd.memset(mhalf[:], -0.5))
            consts["attention"] = n[0]
            step(nc.gpsimd.iota(powers[:, 0:16], pattern=[[16, 16]], base=0, channel_multiplier=0,
                                allow_small_or_imprecise_dtypes=True))
            step(nc.gpsimd.iota(powers[:, 16:32], pattern=[[1, 16]], base=0, channel_multiplier=0,
                                allow_small_or_imprecise_dtypes=True))
            step(nc.gpsimd.iota(nkey[:], pattern=[[0, 1]], base=0, channel_multiplier=-1,
                                allow_small_or_imprecise_dtypes=True))
            for h in range(RH):
                step(nc.gpsimd.memset(gbase[:], 1.0 - 2.0 ** (-5.0 - h)))
                step(nc.gpsimd.tensor_tensor(gpow[:], gbase[:], powers[:], ALU.pow))
                step(nc.gpsimd.tensor_tensor(gkey[:, 0:1], gbase[:, 0:1], nkey[:], ALU.pow))
                step(nc.gpsimd.tensor_scalar(gkey[:, 1:2], gkey[:, 0:1], RK ** -0.5, None, ALU.mult))
                full = decay[:, h, 0:SEQ]
                step(nc.gpsimd.tensor_tensor(
                    full.rearrange("p (a b) -> p a b", a=16),
                    gpow[:, 0:16].unsqueeze(2).to_broadcast([P, 16, 16]),
                    gpow[:, 16:32].unsqueeze(1).to_broadcast([P, 16, 16]), ALU.mult))
                step(nc.gpsimd.tensor_scalar(full, full, gkey[:, 1:2], None, ALU.mult))
                step(nc.gpsimd.affine_select(out=full, in_=full, compare_op=ALU.is_ge, fill=0.0, base=0,
                                             pattern=[[1, SEQ]], channel_multiplier=-1))
                step(nc.gpsimd.tensor_copy(decay[:, h, SEQ:CAUSAL], decay[:, h, 0:P]))
            consts["retention"] = n[0]

            def layer_norm(n):
                for m in range(TT):
                    pool.wait_ge(var_ready, TT * n + m + 1)
                    nc.gpsimd.tensor_tensor(rstd[:, m:m + 1], veps[:, m:m + 1], mhalf[:, 0:1],
                                            ALU.pow).then_inc(rstd_ready, 1)

            def ffn_pair(f, i, z):
                pool.wait_ge(f["gelu_done"], i + 1)
                pool.wait_ge(f["taps_done"], 2 * i + 2)
                if not isinstance(i, int) or i > 0:
                    pool.wait_ge(f["z_ready"], i)
                    pool.wait_ge(f["zh_done"], i)
                nc.gpsimd.tensor_tensor(zf[:], ga[:], ug[:], ALU.mult).then_inc(f["mult_done"], 1)
                pool.wait_ge(f["zh_done"], i + 1)
                nc.gpsimd.tensor_tensor(zl[:, z], zf[:], zh[:, z].bitcast(F32),
                                        ALU.subtract).then_inc(f["z_ready"], 1)

            def ffn_all(l):
                ffn_pair(ffn[l], 0, 0)
                with pool.Fori(1, PAIRS - 1) as i:
                    ffn_pair(ffn[l], i, 0)
                ffn_pair(ffn[l], PAIRS - 1, 1)

            layer_norm(0)
            ffn_all(0)
            layer_norm(1)
            with pool.Fori(0, RH) as h:
                pool.wait_ge(gvar_ready, h + 1)
                nc.gpsimd.tensor_tensor(rstd[:], veps[:], mhalf[:], ALU.pow).then_inc(grstd_ready, 1)
                pool.wait_ge(ro_hi, h + 1)
                nc.gpsimd.tensor_tensor(ol[:, bass.ds(4 * h, 4), :], ygn[:],
                                        oh[:, bass.ds(4 * h, 4), :].bitcast(F32),
                                        ALU.subtract).then_inc(ro_lo, 1)
            layer_norm(2)
            ffn_all(1)
            layer_norm(3)

        @block.scalar
        def _(act):
            def turned_hi(n, tr):
                for m in range(TT):
                    for g in range(2):
                        act.wait_ge(xt_turned, 4 * n + 2 * m + g + 1)
                        nc.scalar.activation(
                            xh[:, 4 * g:4 * g + 4, m * P:(m + 1) * P],
                            ps[:, tr[m][g], :].rearrange("p (k n) -> p k n", k=4), ACT.Copy
                        ).then_inc(xh_ready, 1)

            def q_copy(t):
                act.wait_ge(used, RING * t + 1)
                if not isinstance(t, int) or t > 0:
                    act.wait_ge(s_ready, 4 * t)
                nc.scalar.activation(qT[:], halves(0), ACT.Copy, scale=HD ** -0.5).then_inc(q_copied, 1)

            def k_copy(t):
                act.wait_ge(used, RING * t + 2)
                nc.scalar.activation(kT[:], halves(1), ACT.Copy).then_inc(k_copied, 1)

            def exps(t, h):
                act.wait_ge(max_ready, 4 * t + h + 1)
                for m, (a, b) in enumerate(((0, P), (P, CAUSAL))):
                    last = nc.scalar.activation(sc[:, h % 2, a:b], sc[:, h % 2, a:b], ACT.Exp,
                                                bias=nmax[:, h, m:m + 1], accum_out=rsum[:, h, m:m + 1])
                last.then_inc(exp_ready, 1)

            def pt_copy(t, h):
                act.wait_ge(p_turned, 4 * t + h + 1)
                if h >= 2:
                    act.wait_ge(pv_done, 4 * t + h - 1)
                nc.scalar.activation(pt[:, h % 2, :], ps[:, 5 + h % 2, 0:CAUSAL], ACT.Copy)\
                    .then_inc(pt_ready, 1)

            def out_hi(t, pair):
                act.wait_ge(pv_done, 4 * t + 2 * pair + 2)
                nc.scalar.activation(oh[:, bass.ds(2 * t + pair, 1), :], halves(7)[:, pair:pair + 1, :],
                                     ACT.Copy).then_inc(o_hi, 1)

            def quad(t, core, copies):
                split_hi(act, U_ATT + 2, t)
                exps(core, 0)
                exps(core, 1)
                pt_copy(core, 0)
                split_hi(act, U_ATT + 3, t)
                exps(core, 2)
                pt_copy(core, 1)
                exps(core, 3)
                if copies:
                    q_copy(t)
                pt_copy(core, 2)
                out_hi(core, 0)
                split_hi(act, U_ATT + 4, t)
                if copies:
                    k_copy(t)
                pt_copy(core, 3)
                out_hi(core, 1)

            split_hi(act, 0)
            turned_hi(0, TR_IN)
            split_hi(act, 1)
            split_hi(act, 2)
            split_hi(act, 3)
            q_copy(0)
            split_hi(act, 4)
            k_copy(0)
            act.wait_ge(par_turned, 1)
            nc.scalar.activation(par[:], ps[:, 7, 0:par.shape[1]], ACT.Copy).then_inc(par_copied, 1)
            with act.Fori(1, QUADS) as t:
                quad(t, t - 1, True)
            quad(QUADS, QUADS - 1, False)
            split_hi(act, U_ATT_OUT + 5)
            turned_hi(1, TR_ATT)

            def ffn_conv(l, i, part, u):
                f = ffn[l]
                act.wait_ge(used, up_unit(l, i, part) + RING * i + 1)
                if not isinstance(i, int) or i > 0:
                    act.wait_ge(f["gelu_done"] if part == 0 else f["mult_done"], i)
                if isinstance(i, int) and i == 0 and l == 0 and part == 0:
                    act.wait_ge(par_copied, 1)
                for s in range(2):
                    at = part * (FT // 2) + 2 * i + s
                    nc.scalar.activation(u[:, s, :], up_bank(part, s), ACT.Identity,
                                         bias=par[:, bass.ds(tap(l, 3) + at, 1)],
                                         scale=par[:, bass.ds(tap(l, 2) + at, 1)]).then_inc(f["scaled"], 1)

            def gelu(l, i):
                f = ffn[l]
                act.wait_ge(f["taps_done"], 2 * i + 1)
                if not isinstance(i, int) or i > 0:
                    act.wait_ge(f["mult_done"], i)
                nc.scalar.activation(ga[:], ua[:], ACT.Gelu).then_inc(f["gelu_done"], 1)

            def z_hi(l, i, z):
                f = ffn[l]
                act.wait_ge(f["mult_done"], i + 1)
                if z == 0:
                    act.wait_ge(used, U_FFN[l] + 2 + RING * i)
                nc.scalar.activation(zh[:, z], zf[:], ACT.Copy).then_inc(f["zh_done"], 1)

            def ffn_iter(l, i):
                u = U_FFN[l]
                z_hi(l, i - 1, 0)
                split_hi(act, u + 1, i)
                ffn_conv(l, i, 0, ua)
                split_hi(act, u + 2, i)
                gelu(l, i)
                ffn_conv(l, i, 1, ug)
                split_hi(act, u + 3, i)

            def ffn_all(l):
                split_hi(act, U_FFN[l] + 2)
                ffn_conv(l, 0, 0, ua)
                split_hi(act, U_FFN[l] + 3)
                gelu(l, 0)
                ffn_conv(l, 0, 1, ug)
                with act.Fori(1, PAIRS - 1) as i:
                    ffn_iter(l, i)
                ffn_iter(l, PAIRS - 1)
                z_hi(l, PAIRS - 1, 1)
                split_hi(act, U_FFN[l] + 3 * PAIRS + 1)

            ffn_all(0)
            turned_hi(2, TR_FFN)

            with act.Fori(0, RH) as h:
                split_hi(act, U_RET + 2, 2 * h)
                split_hi(act, U_RET + 3, 2 * h)
                act.wait_ge(used, U_RET + 6 * h + 1)
                nc.scalar.activation(qT[:], halves(0), ACT.Copy).then_inc(rq_copied, 1)
                split_hi(act, U_RET + 4, 2 * h)
                act.wait_ge(used, U_RET + 6 * h + 2)
                nc.scalar.activation(kT[:], halves(1), ACT.Copy).then_inc(rk_copied, 1)
                split_hi(act, U_RET + 5, 2 * h)
                act.wait_ge(used, U_RET + 6 * h + 4)
                nc.scalar.activation(vt[:, 0, :], ps[:, 2, :], ACT.Copy).then_inc(rv_copied[0], 1)
                split_hi(act, U_RET + 6, 2 * h)
                act.wait_ge(used, U_RET + 6 * h + 5)
                nc.scalar.activation(sg[:, 0:2, :], halves(4), ACT.Silu).then_inc(silu_done, 1)
                split_hi(act, U_RET + 7, 2 * h)
                act.wait_ge(used, U_RET + 6 * h + 6)
                nc.scalar.activation(sg[:, 2:4, :], halves(5), ACT.Silu).then_inc(silu_done, 1)
                act.wait_ge(on_turned, h + 1)
                act.wait_ge(ro_lo, h + 1)
                for j in range(4):
                    nc.scalar.activation(ygn[:, j, :], halves(2 + j // 2)[:, j % 2, :], ACT.Identity,
                                         bias=par[:, bass.ds(4 * h + (GN + 2 * KD + j), 1)],
                                         scale=par[:, bass.ds(4 * h + (GN + j), 1)]).then_inc(y_ready, 1)
                act.wait_ge(gated, h + 1)
                nc.scalar.activation(oh[:, bass.ds(4 * h, 4), :], ygn[:], ACT.Copy).then_inc(ro_hi, 1)
            for j in range(8):
                split_hi(act, U_RET_OUT + 2 + j)
            turned_hi(3, TR_RET)
            ffn_all(1)

        @block.vector
        def _(dve):
            def turned_lo(n, tr):
                for m in range(TT):
                    for g in range(2):
                        dve.wait_ge(xh_ready, 4 * n + 2 * m + g + 1)
                        ks, ts = slice(4 * g, 4 * g + 4), slice(m * P, (m + 1) * P)
                        nc.vector.tensor_tensor(
                            xl[:, ks, ts], ps[:, tr[m][g], :].rearrange("p (k n) -> p k n", k=4),
                            xh[:, ks, ts].bitcast(F32), ALU.subtract).then_inc(xl_ready, 1)

            steps = [0]

            def layer_norm(n, acc):
                def step(ins):
                    steps[0] += 1
                    ins.then_inc(dve_ln, 1)

                def settle(but=0):
                    dve.wait_ge(dve_ln, steps[0] - but)

                dve.wait_ge(lnp_loaded[n], 32)
                for m in range(TT):
                    if m == 0:
                        dve.wait_ge(acc_ready, n + 1)
                    else:
                        dve.wait_ge(used, LAST_UNIT[n] + 1)
                    for c in range(2):
                        half = xtok[:, m, c * BANK:(c + 1) * BANK]
                        step(nc.vector.scalar_tensor_tensor(out=half, in0=half, scalar=ALPHA,
                                                            in1=ps[:, acc[m][c], :], op0=ALU.mult, op1=ALU.add))
                    for c in range(2):
                        settle(but=1)
                        step(nc.vector.bn_stats(st6[:, m, c, :], xtok[:, m, c * BANK:(c + 1) * BANK]))
                    settle()
                    step(nc.vector.bn_aggr(mv[:, m, :], st6[:, m].rearrange("p a b -> p (a b)")))
                    settle()
                    nc.vector.tensor_scalar(veps[:, m:m + 1], mv[:, m, 1:2], LN_EPS, None, ALU.add)\
                        .then_inc(var_ready, 1)
                    step(nc.vector.scalar_tensor_tensor(out=xtok[:, m, :], in0=xtok[:, m, :],
                                                        scalar=mv[:, m, 0:1], in1=lnp[:, n % 2, 0, :],
                                                        op0=ALU.subtract, op1=ALU.mult))
                    settle()
                    dve.wait_ge(rstd_ready, TT * n + m + 1)
                    nc.vector.scalar_tensor_tensor(out=xtok[:, m, :], in0=xtok[:, m, :],
                                                   scalar=rstd[:, m:m + 1], in1=lnp[:, n % 2, 1, :],
                                                   op0=ALU.mult, op1=ALU.add).then_inc(x_ready, 1)

            def scores(t, h):
                g = 4 * t + h
                dve.wait_ge(s_ready, g + 1)
                if h >= 2:
                    dve.wait_ge(p_turned, g - 1)
                nc.vector.scalar_tensor_tensor(out=sc[:, h % 2, :], in0=dist[:], scalar=slopes[:, bass.ds(g, 1)],
                                               in1=ps[:, score_bank(t, h), 0:CAUSAL], op0=ALU.mult,
                                               op1=ALU.add).then_inc(biased, 1)
                dve.wait_ge(biased, g + 1)
                for m, (a, b) in enumerate(((0, P), (P, CAUSAL))):
                    last = nc.vector.tensor_reduce(nmax[:, h, m:m + 1], sc[:, h % 2, a:b], AX_X, ALU.max,
                                                   negate=True)
                last.then_inc(max_ready, 1)

            def normalise(t, h):
                g = 4 * t + h
                dve.wait_ge(exp_ready, g + 1)
                nc.vector.reciprocal(rinv[:, h, :], rsum[:, h, :]).then_inc(inv_ready, 1)
                dve.wait_ge(inv_ready, g + 1)
                for m, (a, b) in enumerate(((0, P), (P, CAUSAL))):
                    last = nc.vector.tensor_scalar(sc[:, h % 2, a:b], sc[:, h % 2, a:b], rinv[:, h, m:m + 1],
                                                   None, ALU.mult)
                last.then_inc(p_ready, 1)

            def out_lo(t, pair):
                dve.wait_ge(o_hi, 2 * t + pair + 1)
                at = bass.ds(2 * t + pair, 1)
                nc.vector.tensor_tensor(ol[:, at, :], halves(7)[:, pair:pair + 1, :],
                                        oh[:, at, :].bitcast(F32), ALU.subtract).then_inc(o_lo, 1)

            def v_copy(t):
                dve.wait_ge(used, RING * t + 3)
                if not isinstance(t, int) or t > 0:
                    dve.wait_ge(pv_done, 4 * t)
                nc.vector.tensor_copy(vt[:, :, 0:HALF], halves(2)).then_inc(v_copied, 1)

            def quad(t, core, copies):
                split_lo(dve, U_ATT + 2, t)
                for h in range(2):
                    scores(core, h)
                    normalise(core, h)
                split_lo(dve, U_ATT + 3, t)
                for h in range(2, 4):
                    scores(core, h)
                    normalise(core, h)
                out_lo(core, 0)
                split_lo(dve, U_ATT + 4, t)
                out_lo(core, 1)
                if copies:
                    v_copy(t)

            nc.vector.memset(st6[:], 0.0).then_inc(o_lo, 1)
            nc.vector.memset(mv[:], 0.0).then_inc(ro_lo, 1)
            split_lo(dve, 0)
            turned_lo(0, TR_IN)
            split_lo(dve, 1)
            split_lo(dve, 2)
            split_lo(dve, 3)
            split_lo(dve, 4)
            v_copy(0)
            dve.wait_ge(const_step, consts["attention"])
            with dve.Fori(1, QUADS) as t:
                quad(t, t - 1, True)
            quad(QUADS, QUADS - 1, False)
            split_lo(dve, U_ATT_OUT + 5)
            layer_norm(0, ACC_ATT)
            turned_lo(1, TR_ATT)

            def ffn_taps(l, i, part, u):
                f = ffn[l]
                for back in (1, 2):
                    for s in range(2):
                        if back == 1:
                            dve.wait_ge(f["scaled"], 4 * i + 2 * part + s + 1)
                        else:
                            dve.wait_ge(f["tap1"], 4 * i + 2 * part + s + 1)
                        at = part * (FT // 2) + 2 * i + s
                        ins = nc.vector.scalar_tensor_tensor(
                            out=u[:, s, back:SEQ], in0=up_bank(part, s)[:, 0:SEQ - back],
                            scalar=par[:, bass.ds(tap(l, 2 - back) + at, 1)], in1=u[:, s, back:SEQ],
                            op0=ALU.mult, op1=ALU.add)
                        if back == 1:
                            ins.then_inc(f["tap1"], 1)
                ins.then_inc(f["taps_done"], 1)

            def ffn_iter(l, i):
                u = U_FFN[l]
                split_lo(dve, u + 1, i)
                ffn_taps(l, i, 0, ua)
                split_lo(dve, u + 2, i)
                ffn_taps(l, i, 1, ug)
                split_lo(dve, u + 3, i)

            def ffn_all(l):
                split_lo(dve, U_FFN[l] + 2)
                ffn_taps(l, 0, 0, ua)
                split_lo(dve, U_FFN[l] + 3)
                ffn_taps(l, 0, 1, ug)
                with dve.Fori(1, PAIRS - 1) as i:
                    ffn_iter(l, i)
                ffn_iter(l, PAIRS - 1)
                split_lo(dve, U_FFN[l] + 3 * PAIRS + 1)

            ffn_all(0)
            layer_norm(1, ACC_FFN)
            turned_lo(2, TR_FFN)

            GN_STEPS = TT + 2
            dve.wait_ge(const_step, consts["retention"])
            with dve.Fori(0, RH) as h:
                for j in range(2, 6):
                    split_lo(dve, U_RET + j, 2 * h)
                dve.wait_ge(used, U_RET + 6 * h + 4)
                nc.vector.tensor_copy(vt[:, 1, :], ps[:, 3, :]).then_inc(rv_copied[1], 1)
                dve.wait_ge(rs_ready, h + 1)
                nc.vector.tensor_tensor(pt[:, 0:1, :], ps[:, 6:7, 0:CAUSAL], decay[:, bass.ds(h, 1), :],
                                        ALU.mult).then_inc(decayed, 1)
                split_lo(dve, U_RET + 6, 2 * h)
                split_lo(dve, U_RET + 7, 2 * h)
                for m, bank in enumerate((7, 0)):
                    dve.wait_ge(ro_ready, TT * h + m + 1)
                    nc.vector.bn_stats(st6[:, m, 0, :], ps[:, bank, :]).then_inc(dve_gn, 1)
                st = [st6[:, :, 0, i] for i in range(6)]
                dve.wait_ge(dve_gn, GN_STEPS * h + TT)
                nc.vector.tensor_tensor(gm[:, 0, :], st[1], st[4], ALU.add)
                nc.vector.tensor_tensor(gm[:, 1, :], st[1], st[4], ALU.subtract)
                nc.vector.tensor_tensor(gm[:, 2, :], st[2], st[5], ALU.add).then_inc(dve_gn, 1)
                dve.wait_ge(dve_gn, GN_STEPS * h + TT + 1)
                nc.vector.tensor_scalar(gmean[:], gm[:, 0, :], 0.5, None, ALU.mult)
                nc.vector.scalar_tensor_tensor(out=gm[:, 3, :], in0=gm[:, 1, :], scalar=0.25, in1=gm[:, 1, :],
                                               op0=ALU.mult, op1=ALU.mult)
                nc.vector.tensor_scalar(gm[:, 4, :], gm[:, 2, :], 1.0 / RV, GN_EPS, ALU.mult, ALU.add)\
                    .then_inc(dve_gn, 1)
                dve.wait_ge(dve_gn, GN_STEPS * h + TT + 2)
                nc.vector.tensor_tensor(veps[:], gm[:, 3, :], gm[:, 4, :], ALU.add).then_inc(gvar_ready, 1)
                dve.wait_ge(grstd_ready, h + 1)
                for m, bank in enumerate((7, 0)):
                    nc.vector.tensor_scalar(onrm[:, m, :], ps[:, bank, :], gmean[:, m:m + 1], rstd[:, m:m + 1],
                                            ALU.subtract, ALU.mult).then_inc(on_ready, 1)
                dve.wait_ge(y_ready, 4 * h + 4)
                dve.wait_ge(silu_done, 2 * h + 2)
                nc.vector.tensor_tensor(ygn[:], ygn[:], sg[:], ALU.mult).then_inc(gated, 1)
            for j in range(8):
                split_lo(dve, U_RET_OUT + 2 + j)
            layer_norm(2, ACC_RET)
            turned_lo(3, TR_RET)
            ffn_all(1)
            layer_norm(3, ACC_FFN)

        @block.tensor
        def _(pe):
            def turn_x(n, m, tr):
                for g in range(2):
                    for k in range(4):
                        last = nc.tensor.transpose(ps[:, tr[m][g], k * P:(k + 1) * P],
                                                   xtok[:, m, (4 * g + k) * P:(4 * g + k + 1) * P], ident[:])
                    last.then_inc(xt_turned, 1)

            def turn_after_ln(n, tr):
                for m in range(TT):
                    pe.wait_ge(x_ready, TT * n + m + 1)
                    turn_x(n, m, tr)
                pe.wait_ge(xl_ready, 4 * (n + 2))

            def project_chunk(t, x_):
                u, j, half = x_ // 4, x_ // 2 % 2, x_ % 2
                if x_ % 4 == 0:
                    unit_ready(pe, U_ATT + u, t)
                    if not isinstance(t, int) or t > 0:
                        pe.wait_ge((q_copied, k_copied, v_copied)[u], t)
                ks = range(4 * half, 4 * half + 4)
                if u < 2:
                    last = feature_tile(halves(u)[:, j, :], u, j, ks)
                else:
                    h, l = cols(whi, u), cols(wlo, u)
                    for k in ks:
                        last = products(halves(2)[:, j, :], xh[:, k, j * P:(j + 1) * P],
                                        xl[:, k, j * P:(j + 1) * P], h[:, k, :], l[:, k, :],
                                        k == 0, k == KD - 1)
                if x_ % 4 == 3:
                    last.then_inc(used, 1)

            def head_rows(h):
                return slice(HD * (h % 2), HD * (h % 2) + HD), h // 2

            def score(t, h):
                rs, pair = head_rows(h)
                if h == 0:
                    pe.wait_ge(q_copied, t + 1)
                    pe.wait_ge(k_copied, t + 1)
                if isinstance(t, int) and t == QUADS - 1:
                    if h >= 1:
                        pe.wait_ge(biased, 4 * t + h)
                elif h >= 2:
                    pe.wait_ge(biased, 4 * t + h - 1)
                bank = ps[:, score_bank(t, h), :]
                nc.tensor.matmul(bank[:, 0:P], qT[rs, pair, 0:P], kT[rs, pair, 0:P], start=True, stop=True)
                nc.tensor.matmul(bank[:, P:CAUSAL], qT[rs, pair, P:SEQ], kT[rs, pair, :],
                                 start=True, stop=True).then_inc(s_ready, 1)

            def turn_p(t, h):
                pe.wait_ge(p_ready, 4 * t + h + 1)
                for b in range(3):
                    last = nc.tensor.transpose(ps[:, 5 + h % 2, b * P:(b + 1) * P],
                                               sc[:, h % 2, b * P:(b + 1) * P], ident[:])
                last.then_inc(p_turned, 1)

            def values(t, h):
                rs, pair = head_rows(h)
                pe.wait_ge(pt_ready, 4 * t + h + 1)
                if h == 0:
                    pe.wait_ge(v_copied, t + 1)
                    pe.wait_ge(o_lo, 2 * t + 1)
                if h == 2:
                    pe.wait_ge(o_lo, 2 * t + 2)
                dst = halves(7)[rs, pair, :]
                nc.tensor.matmul(dst, vt[:, 0, h * HD:(h + 1) * HD], pt[:, h % 2, 0:SEQ], start=True, stop=False)
                nc.tensor.matmul(dst[:, P:SEQ], vt[:, 1, h * HD:(h + 1) * HD], pt[:, h % 2, SEQ:CAUSAL],
                                 start=False, stop=True).then_inc(pv_done, 1)

            def core(t, x_):
                for h in range(4):
                    if x_ == 2 * h:
                        score(t, h)
                    if x_ == 2 * h + 3:
                        turn_p(t, h)
                    if x_ == 2 * h + 5:
                        values(t, h)

            pe.wait_ge(const_step, 2)
            pe.wait_ge(x_loaded, 16)
            for m in range(TT):
                turn_x(0, m, TR_IN)
            pe.wait_ge(xl_ready, 4)
            for x_ in range(12):
                project_chunk(0, x_)
            pe.wait_ge(par_loaded, 16 * 6)
            for i in range(8):
                nc.tensor.transpose(ps[:, 7, i * FT:(i + 1) * FT], stage[:, i, :], ident[0:FT, 0:FT])
            for i in range(2):
                last = nc.tensor.transpose(ps[:, 7, GN + i * 2 * KD:GN + (i + 1) * 2 * KD], gstage[:, i, :],
                                           ident[0:2 * KD, 0:2 * KD])
            last.then_inc(par_turned, 1)
            pe.wait_ge(par_copied, 1)
            with pe.Fori(1, QUADS) as t:
                for x_ in range(12):
                    core(t - 1, x_)
                    project_chunk(t, x_)
            for name in (q_copied, k_copied, v_copied):
                pe.wait_ge(name, QUADS)
            for j in range(4):
                c = U_ATT_OUT + j
                for x_ in range(4):
                    if j < 3:
                        core(QUADS - 1, 4 * j + x_)
                    if x_ == 0:
                        unit_ready(pe, c)
                        pe.wait_ge(o_lo, 7 if j < 3 else 9)
                    m, kk = x_ // 2, x_ % 2
                    k = 2 * j + kk
                    last = out_rows(ACC_ATT, oh[:, k, :], ol[:, k, :], c, m, kk, k == 0, k == KD - 1)
                    if j == 3 and x_ == 1:
                        last.then_inc(acc_ready, 1)
                last.then_inc(used, 1)
            turn_after_ln(0, TR_ATT)

            def up_pair(l, i, part):
                c = up_unit(l, i, part)
                unit_ready(pe, c, i)
                if not isinstance(i, int) or i > 0:
                    pe.wait_ge(ffn[l]["taps_done"], 2 * i + part - 1)
                feature_tile(up_bank(part, 0), c, 0)
                feature_tile(up_bank(part, 1), c, 1).then_inc(used, 1)

            def down_pair(l, c, i, pair, z=0, first=False, last=False):
                unit_ready(pe, c, i)
                pe.wait_ge(ffn[l]["z_ready"], pair + 1)
                for m in range(TT):
                    for kk in range(2):
                        ins = out_rows(ACC_FFN, zh[:, z, kk, :], zl[:, z, kk, :], c, m, kk,
                                       first and kk == 0, last and kk == 1)
                    if last and m == 0:
                        ins.then_inc(acc_ready, 1)
                ins.then_inc(used, 1)

            def ffn_iter(l, i, first=False):
                up_pair(l, i, 0)
                up_pair(l, i, 1)
                down_pair(l, U_FFN[l] + 1, i, i - 1, first=first)

            def ffn_all(l):
                up_pair(l, 0, 0)
                up_pair(l, 0, 1)
                ffn_iter(l, 1, first=True)
                with pe.Fori(2, PAIRS - 1) as i:
                    ffn_iter(l, i)
                ffn_iter(l, PAIRS - 1)
                down_pair(l, U_FFN[l] + 3 * PAIRS - 1, 0, PAIRS - 1, z=1, last=True)

            ffn_all(0)
            turn_after_ln(1, TR_FFN)

            with pe.Fori(0, RH) as h:
                for j in range(2):
                    unit_ready(pe, U_RET + j, 2 * h)
                    feature_tile(halves(j)[:, 0, :], U_RET + j, 0)
                    feature_tile(halves(j)[:, 1, :], U_RET + j, 1).then_inc(used, 1)
                pe.wait_ge(rq_copied, h + 1)
                for j in range(2):
                    c = U_RET + 2 + j
                    unit_ready(pe, c, 2 * h)
                    wh, wl = quarter(whi, c % RING), quarter(wlo, c % RING)
                    for m in range(TT):
                        for kk in range(4):
                            k = 4 * j + kk
                            last = products(ps[:, 2 + m, :], xh[:, k, m * P:(m + 1) * P],
                                            xl[:, k, m * P:(m + 1) * P], wh[:, kk, :], wl[:, kk, :],
                                            k == 0, k == KD - 1)
                    last.then_inc(used, 1)
                pe.wait_ge(rk_copied, h + 1)
                for m, (a, b) in enumerate(((0, SEQ), (SEQ, CAUSAL))):
                    for k in range(2):
                        last = nc.tensor.matmul(ps[:, 6, a:b], kT[:, k, m * P:(m + 1) * P],
                                                qT[:, k, m * P:SEQ], start=k == 0, stop=k == 1)
                last.then_inc(rs_ready, 1)
                for j in range(2):
                    c = U_RET + 4 + j
                    unit_ready(pe, c, 2 * h)
                    feature_tile(halves(4 + j)[:, 0, :], c, 0)
                    feature_tile(halves(4 + j)[:, 1, :], c, 1).then_inc(used, 1)
                    if j == 0:
                        pe.wait_ge(decayed, h + 1)
                        pe.wait_ge(rv_copied[0], h + 1)
                        pe.wait_ge(rv_copied[1], h + 1)
                        nc.tensor.matmul(ps[:, 7, :], pt[:, 0, 0:P], vt[:, 0, :], start=True, stop=True)\
                            .then_inc(ro_ready, 1)
                        nc.tensor.matmul(ps[:, 0, :], pt[:, 0, P:SEQ], vt[:, 0, :], start=True, stop=False)
                        nc.tensor.matmul(ps[:, 0, :], pt[:, 0, SEQ:CAUSAL], vt[:, 1, :], start=False, stop=True)\
                            .then_inc(ro_ready, 1)
                for m in range(TT):
                    pe.wait_ge(on_ready, TT * h + m + 1)
                    for j in range(4):
                        last = nc.tensor.transpose(halves(2 + j // 2)[:, j % 2, m * P:(m + 1) * P],
                                                   onrm[:, m, j * P:(j + 1) * P], ident[:])
                last.then_inc(on_turned, 1)

            pe.wait_ge(silu_done, 2 * RH)
            for j in range(8):
                c = U_RET_OUT + j
                unit_ready(pe, c)
                pe.wait_ge(ro_lo, j // 2 + 2)
                for m in range(TT):
                    for kk in range(2):
                        k = 2 * j + kk
                        last = out_rows(ACC_RET, oh[:, k, :], ol[:, k, :], c, m, kk, k == 0, k == 2 * KD - 1)
                    if j == 7 and m == 0:
                        last.then_inc(acc_ready, 1)
                last.then_inc(used, 1)
            turn_after_ln(2, TR_RET)
            ffn_all(1)


_INS = ["x", "att_w_in", "att_w_out", "ret_w_in", "ret_w_out", "ret_gn_g", "ret_gn_b", "mix_ln_g",
        "mix_ln_b", "ffn_ln_g", "ffn_ln_b", "ffn_w_up", "ffn_conv_w", "ffn_conv_b", "ffn_w_down"]
_OUTS = [((1, SEQ, D), "float32")]


def kernel(**inputs):
    import numpy as _np
    import concourse.bacc as _bacc
    from concourse import mybir as _mybir
    from concourse.bass_utils import run_bass_kernel_spmd as _run

    nc = _bacc.Bacc("TRN2", target_bir_lowering=False, num_devices=1)
    arrays, args = {}, []
    for name in _INS:
        a = _np.ascontiguousarray(inputs[name])
        arrays[f"in_{name}_dram"] = a
        args.append(nc.dram_tensor(f"in_{name}_dram", a.shape, _mybir.dt.from_np(a.dtype), kind="ExternalInput").ap())
    for i, (shape, dtype) in enumerate(_OUTS):
        dt = _mybir.dt.from_np(_np.dtype(dtype))
        args.append(nc.dram_tensor(f"out_{i}_dram", shape, dt, kind="ExternalOutput").ap())
    decoder_trunk(nc, *args)
    r = _run(nc, [arrays], core_ids=[0])
    got = tuple(r.results[0][f"out_{i}_dram"] for i in range(len(_OUTS)))
    return got[0]
```

```python
from contextlib import ExitStack

import concourse.bass as bass
from concourse import mybir

F32 = mybir.dt.float32
F32R = mybir.dt.float32r
ALU = mybir.AluOpType
ACT = mybir.ActivationFunctionType
AX_X = mybir.AxisListType.X

P = 128
SEQ = 256
TT = SEQ // P
D = 1024
KD = D // P
HEADS = 16
HD = D // HEADS
QUADS = 4
RH = 4
RK = D // RH
RV = 2 * RK
FFN = 2816
FT = 2 * FFN // P
PAIRS = FFN // 256
UNIT = 2048
RING = 3
HALF = 256
BANK = 512
LN_EPS = 1e-5
GN_EPS = 1e-5
ALPHA = (2.0 * 2) ** 0.25
MASKED = -1e33
CAUSAL = P + SEQ

U_ATT = 0
U_ATT_OUT = U_ATT + 3 * QUADS
U_FFN = [U_ATT_OUT + 4, 0]
U_RET = U_FFN[0] + 3 * PAIRS
U_RET_OUT = U_RET + 6 * RH
U_FFN[1] = U_RET_OUT + 8
UNITS = U_FFN[1] + 3 * PAIRS
LAST_UNIT = [U_FFN[0] - 1, U_RET - 1, U_FFN[1] - 1, UNITS - 1]

ACC_ATT, TR_ATT = [[0, 1], [2, 4]], [[5, 6], [7, 3]]
ACC_FFN, TR_FFN = [[2, 3], [0, 1]], [[6, 7], [4, 5]]
ACC_RET, TR_RET = [[1, 6], [4, 5]], [[2, 3], [0, 7]]
TR_IN = [[0, 1], [2, 3]]


def decoder_trunk(nc, x, att_w_in, att_w_out, ret_w_in, ret_w_out, ret_gn_g, ret_gn_b, mix_ln_g,
                  mix_ln_b, ffn_ln_g, ffn_ln_b, ffn_w_up, ffn_conv_w, ffn_conv_b, ffn_w_down, out):
    with ExitStack() as ctx:
        def sb(name, shape, dt=F32):
            return ctx.enter_context(nc.sbuf_tensor(name, shape, dt))

        def sem(name):
            return ctx.enter_context(nc.semaphore(name))

        raw = sb("raw", [P, RING, UNIT])
        whi = sb("whi", [P, RING, UNIT], F32R)
        wlo = sb("wlo", [P, RING, UNIT], F32R)
        xtok = sb("xtok", [P, TT, D])
        xh = sb("xh", [P, KD, SEQ], F32R)
        xl = sb("xl", [P, KD, SEQ], F32R)
        oh = sb("oh", [P, 2 * KD, SEQ], F32R)
        ol = sb("ol", [P, 2 * KD, SEQ], F32R)
        lnp = sb("lnp", [P, 2, 2, D])
        par = sb("par", [P, 8 * FT + 2 * 2 * KD])
        ident = sb("ident", [P, P])
        dist = sb("dist", [P, CAUSAL])
        slopes = sb("slopes", [P, HEADS])
        decay = sb("decay", [P, RH, CAUSAL])
        powers = sb("powers", [P, 32])
        gbase = sb("gbase", [P, 32])
        gpow = sb("gpow", [P, 32])
        gkey = sb("gkey", [P, 2])
        nkey = sb("nkey", [P, 1])
        mhalf = sb("mhalf", [P, TT])
        gm = sb("gm", [P, 5, TT])
        gmean = sb("gmean", [P, TT])
        st6 = sb("st6", [P, TT, 2, 6])
        half_sum = sb("half_sum", [P, TT, 2])
        nmean = sb("nmean", [P, TT])
        var = sb("var", [P, TT])
        lnt = sb("lnt", [P, TT, D])
        stage = lnt[0:FT, 0, :].rearrange("f (w n) -> f w n", w=8)
        gstage = lnt[0:2 * KD, 1, 0:2 * P].rearrange("f (w n) -> f w n", w=2)
        veps = sb("veps", [P, TT])
        rstd = sb("rstd", [P, TT])
        qT = sb("qT", [P, 2, SEQ])
        kT = sb("kT", [P, 2, SEQ])
        vt = sb("vt", [P, TT, BANK])
        sc = sb("sc", [P, 2, CAUSAL])
        pt = sb("pt", [P, 2, CAUSAL])
        nmax = sb("nmax", [P, 4, TT])
        rsum = sb("rsum", [P, 4, TT])
        rinv = sb("rinv", [P, 4, TT])
        ua = sb("ua", [P, 2, SEQ])
        ug = sb("ug", [P, 2, SEQ])
        ga = sb("ga", [P, 2, SEQ])
        zf = sb("zf", [P, 2, SEQ])
        zh = sb("zh", [P, 2, 2, SEQ], F32R)
        zl = sb("zl", [P, 2, 2, SEQ], F32R)
        onrm = sb("onrm", [P, TT, RV])
        squares = onrm[:, :, :].rearrange("p m n -> p (m n)")
        ygn = sb("ygn", [P, 4, SEQ])
        sg = sb("sg", [P, 4, SEQ])
        ps = ctx.enter_context(nc.psum_tensor("ps", [P, 8, BANK], F32))

        x_loaded = [sem(f"x_loaded{m}") for m in range(TT)]
        first_loaded = [sem(f"first_loaded{i}") for i in range(2)]
        first_hi = sem("first_hi")
        first_lo = sem("first_lo")
        par_loaded = sem("par_loaded")
        lnp_loaded = [sem(f"lnp_loaded{i}") for i in range(4)]
        loaded = [sem(f"loaded{i}") for i in range(RING)]
        hi_done = sem("hi_done")
        lo_done = sem("lo_done")
        lo_half = sem("lo_half")
        used = sem("used")
        stored = sem("stored")
        const_step = sem("const_step")
        par_turned = sem("par_turned")
        par_copied = sem("par_copied")
        acc_ready = sem("acc_ready")
        dve_ln = sem("dve_ln")
        mean_ready = sem("mean_ready")
        var_ready = sem("var_ready")
        veps_ready = sem("veps_ready")
        rstd_ready = sem("rstd_ready")
        x_ready = sem("x_ready")
        xt_turned = sem("xt_turned")
        xh_ready = sem("xh_ready")
        xl_ready = sem("xl_ready")
        q_copied = sem("q_copied")
        k_copied = sem("k_copied")
        v_copied = sem("v_copied")
        s_ready = sem("s_ready")
        biased = sem("biased")
        max_ready = sem("max_ready")
        exp_ready = sem("exp_ready")
        inv_ready = sem("inv_ready")
        p_ready = sem("p_ready")
        p_turned = sem("p_turned")
        pt_ready = sem("pt_ready")
        pv_done = sem("pv_done")
        o_hi = sem("o_hi")
        o_lo = sem("o_lo")
        rq_copied = sem("rq_copied")
        rk_copied = sem("rk_copied")
        rv_copied = [sem(f"rv_copied{m}") for m in range(TT)]
        rs_ready = sem("rs_ready")
        decayed = sem("decayed")
        ro_ready = sem("ro_ready")
        dve_gn = sem("dve_gn")
        gvar_ready = sem("gvar_ready")
        grstd_ready = sem("grstd_ready")
        on_ready = sem("on_ready")
        on_turned = sem("on_turned")
        y_ready = sem("y_ready")
        silu_done = sem("silu_done")
        gated = sem("gated")
        ro_hi = sem("ro_hi")
        ro_lo = sem("ro_lo")
        ffn = [{n: sem(f"{n}_{l}") for n in (
            "scaled", "tap1", "taps_done", "gelu_done", "mult_done", "zh_done", "z_ready",
            "last_gate", "last_taps")}
            for l in range(2)]

        def cols(t, slot):
            return t[:, slot].rearrange("p (k n) -> p k n", k=KD)

        def rows(t, slot):
            return t[:, slot].rearrange("p (k n) -> p k n", k=2)

        def quarter(t, slot):
            return t[:, slot].rearrange("p (k n) -> p k n", k=4)

        def halves(bank):
            return ps[:, bank, :].rearrange("p (j n) -> p j n", j=2)

        def up_bank(part, s):
            return ps[:, 4 + 2 * part + s, 0:SEQ]

        def tap(l, w):
            return (4 * l + w) * FT

        def up_unit(l, i, part):
            return U_FFN[l] + part if isinstance(i, int) and i == 0 else U_FFN[l] - 1 + part

        def score_bank(t, h):
            return (3, 5)[h % 2] if isinstance(t, int) and t == QUADS - 1 else 3 + h % 2

        GN = 8 * FT

        def load(sp, c, i, view, src):
            s = c % RING
            if not (isinstance(i, int) and c + RING * i < RING):
                sp.wait_ge(lo_done, c + RING * i - RING + 1)
            sp.dma_start(view(raw, s), src).then_inc(loaded[s], 16)

        def split_hi(act, c, i=0):
            if isinstance(i, int) and c + RING * i >= UNITS:
                return
            s = c % RING
            act.wait_ge(loaded[s], 16 * (c // RING + i + (s != 0)))
            if not (isinstance(i, int) and c + RING * i < RING):
                act.wait_ge(used, c + RING * i - RING + 1)
            nc.scalar.activation(whi[:, s], raw[:, s], ACT.Copy).then_inc(hi_done, 1)

        def split_lo(dve, c, i=0):
            if isinstance(i, int) and c + RING * i >= UNITS:
                return
            s = c % RING
            dve.wait_ge(hi_done, c + RING * i + 1)
            nc.vector.tensor_tensor(wlo[:, s], raw[:, s], whi[:, s].bitcast(F32),
                                    ALU.subtract).then_inc(lo_done, 1)

        shared = [U_FFN[0] + 3 * PAIRS - 1, U_RET + 1, U_FFN[1] + 3 * PAIRS - 1]

        def share_lo(eng, tensor_tensor, c, half, first):
            n, s, b = shared.index(c) + 1, c % RING, slice(half * (UNIT // 2), (half + 1) * (UNIT // 2))
            eng.wait_ge(hi_done, c + 1)
            if first:
                eng.wait_ge(lo_done, c)
                tensor_tensor(wlo[:, s, b], raw[:, s, b], whi[:, s, b].bitcast(F32),
                              ALU.subtract).then_inc(lo_half, 1)
            else:
                eng.wait_ge(lo_half, n)
                tensor_tensor(wlo[:, s, b], raw[:, s, b], whi[:, s, b].bitcast(F32),
                              ALU.subtract).then_inc(lo_done, 1)

        def products(dst, ah, al, bh, bl, start, stop):
            nc.tensor.matmul(dst, ah, bh, start=start, stop=False)
            nc.tensor.matmul(dst, ah, bl, start=False, stop=False)
            return nc.tensor.matmul(dst, al, bh, start=False, stop=stop)

        def unit_ready(pe, c, i=0):
            pe.wait_ge(lo_done, c + RING * i + 1)

        def feature_tile(dst, c, j, ks=range(KD)):
            h, l = cols(whi, c % RING), cols(wlo, c % RING)
            for k in ks:
                last = products(dst, h[:, k, j * P:(j + 1) * P], l[:, k, j * P:(j + 1) * P],
                                xh[:, k, :], xl[:, k, :], k == 0, k == KD - 1)
            return last

        def out_rows(acc, ah, al, c, m, kk, first, last, columns=range(2)):
            h, l = rows(whi, c % RING), rows(wlo, c % RING)
            for n in columns:
                b = slice(n * BANK, (n + 1) * BANK)
                ins = products(ps[:, acc[m][n], :], ah[:, m * P:(m + 1) * P], al[:, m * P:(m + 1) * P],
                               h[:, kk, b], l[:, kk, b], first, last)
            return ins

        consts = {}

        block = ctx.enter_context(nc.Block())

        @block.sync
        def _(sp):
            def in_cols(w, at):
                return w[:, bass.ds(at, 256)].rearrange("(k p) n -> p k n", p=P)

            def in_rows(w, at):
                return w[bass.ds(at, 256), :].rearrange("(k p) n -> p k n", p=P)

            def ln_params(slot, n, g, b):
                for i, v in enumerate((g, b)):
                    sp.dma_start(lnp[:, slot, i, :], v.partition_broadcast(P)).then_inc(lnp_loaded[n], 16)

            for m in range(TT):
                sp.dma_start(xtok[:, m, :], x[0, m * P:(m + 1) * P, :]).then_inc(x_loaded[m], 16)
            for i in range(2):
                sp.dma_start(cols(raw, 0)[:, 4 * i:4 * i + 4, :],
                             att_w_in[0, i * BANK:(i + 1) * BANK, 0:256].rearrange("(k p) n -> p k n", p=P))\
                  .then_inc(first_loaded[i], 16)
            for j in range(1, 3):
                load(sp, j, 0, cols, in_cols(att_w_in[0], j * D))
            for l in range(2):
                sp.dma_start(stage[:, 4 * l:4 * l + 3, :],
                             ffn_conv_w[l].rearrange("w (f p) -> f w p", p=P)).then_inc(par_loaded, 16)
                sp.dma_start(stage[:, 4 * l + 3, :],
                             ffn_conv_b[l].rearrange("(f p) -> f p", p=P)).then_inc(par_loaded, 16)
            for i, v in enumerate((ret_gn_g, ret_gn_b)):
                sp.dma_start(gstage[:, i, :], v[0].rearrange("(f p) -> f p", p=P)).then_inc(par_loaded, 16)
            with sp.Fori(1, QUADS) as t:
                for j in range(3):
                    load(sp, j, t, cols, in_cols(att_w_in[0], t * 256 + j * D))
            ln_params(0, 0, mix_ln_g[0], mix_ln_b[0])
            for j in range(4):
                load(sp, U_ATT_OUT + j, 0, rows, in_rows(att_w_out[0], j * 256))
            ln_params(1, 1, ffn_ln_g[0], ffn_ln_b[0])

            def ffn_loads(l):
                u = U_FFN[l]
                load(sp, u, 0, cols, in_cols(ffn_w_up[l], 0))
                load(sp, u + 1, 0, cols, in_cols(ffn_w_up[l], FFN))
                with sp.Fori(1, PAIRS) as i:
                    load(sp, u - 1, i, cols, in_cols(ffn_w_up[l], i * 256))
                    load(sp, u, i, cols, in_cols(ffn_w_up[l], i * 256 + FFN))
                    load(sp, u + 1, i, rows, in_rows(ffn_w_down[l], i * 256 - 256))
                load(sp, u + 3 * PAIRS - 1, 0, rows, in_rows(ffn_w_down[l], FFN - 256))

            ffn_loads(0)
            sp.wait_ge(x_ready, 4)
            ln_params(0, 2, mix_ln_g[1], mix_ln_b[1])
            with sp.Fori(0, RH) as h:
                for j in range(2):
                    load(sp, U_RET + j, 2 * h, quarter,
                         ret_w_in[0][j * BANK:(j + 1) * BANK, bass.ds(h * RV + 2 * D, RV)]
                         .rearrange("(k p) n -> p k n", p=P))
                for j in range(2):
                    load(sp, U_RET + 2 + j, 2 * h, cols, in_cols(ret_w_in[0], h * RK + j * D))
                for j in range(2):
                    load(sp, U_RET + 4 + j, 2 * h, cols, in_cols(ret_w_in[0], h * RV + 4 * D + j * 256))
            for j in range(8):
                load(sp, U_RET_OUT + j, 0, rows, in_rows(ret_w_out[0], j * 256))
            sp.wait_ge(x_ready, 8)
            ln_params(1, 3, ffn_ln_g[1], ffn_ln_b[1])
            ffn_loads(1)
            for m in range(TT):
                for c in range(2):
                    sp.wait_ge(x_ready, 12 + 2 * m + c + 1)
                    b = slice(c * BANK, (c + 1) * BANK)
                    sp.dma_start(out[0, m * P:(m + 1) * P, b], xtok[:, m, b]).then_inc(stored, 16)
            sp.wait_ge(stored, 16 * 2 * TT)

        @block.gpsimd
        def _(pool):
            n = [0]

            def step(ins):
                n[0] += 1
                ins.then_inc(const_step, 1)
                pool.wait_ge(const_step, n[0])

            step(nc.gpsimd.memset(ident[:], 0.0))
            step(nc.gpsimd.affine_select(out=ident[:], in_=ident[:], compare_op=ALU.not_equal, fill=1.0,
                                         base=0, pattern=[[-1, P]], channel_multiplier=1))
            for m, (a, b) in enumerate(((0, P), (P, CAUSAL))):
                step(nc.gpsimd.iota(dist[:, a:b], pattern=[[1, b - a]], base=-m * P, channel_multiplier=-1,
                                    allow_small_or_imprecise_dtypes=True))
                step(nc.gpsimd.affine_select(out=dist[:, a:b], in_=dist[:, a:b], compare_op=ALU.is_ge,
                                             fill=MASKED, base=m * P, pattern=[[-1, b - a]],
                                             channel_multiplier=1))
            for h in range(HEADS):
                nc.gpsimd.memset(slopes[:, h:h + 1], 2.0 ** (-8.0 * (h + 1) / HEADS))
            step(nc.gpsimd.memset(mhalf[:], -0.5))
            consts["attention"] = n[0]
            step(nc.gpsimd.iota(powers[:, 0:16], pattern=[[16, 16]], base=0, channel_multiplier=0,
                                allow_small_or_imprecise_dtypes=True))
            step(nc.gpsimd.iota(powers[:, 16:32], pattern=[[1, 16]], base=0, channel_multiplier=0,
                                allow_small_or_imprecise_dtypes=True))
            step(nc.gpsimd.iota(nkey[:], pattern=[[0, 1]], base=0, channel_multiplier=-1,
                                allow_small_or_imprecise_dtypes=True))
            for h in range(RH):
                step(nc.gpsimd.memset(gbase[:], 1.0 - 2.0 ** (-5.0 - h)))
                step(nc.gpsimd.tensor_tensor(gpow[:], gbase[:], powers[:], ALU.pow))
                step(nc.gpsimd.tensor_tensor(gkey[:, 0:1], gbase[:, 0:1], nkey[:], ALU.pow))
                step(nc.gpsimd.tensor_scalar(gkey[:, 1:2], gkey[:, 0:1], RK ** -0.5, None, ALU.mult))
                full = decay[:, h, 0:SEQ]
                step(nc.gpsimd.tensor_tensor(
                    full.rearrange("p (a b) -> p a b", a=16),
                    gpow[:, 0:16].unsqueeze(2).to_broadcast([P, 16, 16]),
                    gpow[:, 16:32].unsqueeze(1).to_broadcast([P, 16, 16]), ALU.mult))
                step(nc.gpsimd.tensor_scalar(full, full, gkey[:, 1:2], None, ALU.mult))
                step(nc.gpsimd.affine_select(out=full, in_=full, compare_op=ALU.is_ge, fill=0.0, base=0,
                                             pattern=[[1, SEQ]], channel_multiplier=-1))
                step(nc.gpsimd.tensor_copy(decay[:, h, SEQ:CAUSAL], decay[:, h, 0:P]))
            consts["retention"] = n[0]

            def inverse_root(n):
                for m in range(TT):
                    if (n, m) == (1, 1):
                        share_lo(pool, nc.gpsimd.tensor_tensor, U_RET + 1, 0, first=True)
                    pool.wait_ge(veps_ready, TT * n + m + 1)
                    nc.gpsimd.tensor_tensor(rstd[:, m:m + 1], veps[:, m:m + 1], mhalf[:, 0:1],
                                            ALU.pow).then_inc(rstd_ready, 1)

            def ffn_pair(f, i):
                pool.wait_ge(f["gelu_done"], i + 1)
                pool.wait_ge(f["taps_done"], 2 * i + 2)
                if not isinstance(i, int) or i > 0:
                    pool.wait_ge(f["z_ready"], i)
                    pool.wait_ge(f["zh_done"], i)
                nc.gpsimd.tensor_tensor(zf[:], ga[:], ug[:], ALU.mult).then_inc(f["mult_done"], 1)
                pool.wait_ge(f["zh_done"], i + 1)
                nc.gpsimd.tensor_tensor(zl[:, 0], zf[:], zh[:, 0].bitcast(F32),
                                        ALU.subtract).then_inc(f["z_ready"], 1)

            def ffn_all(l):
                ffn_pair(ffn[l], 0)
                with pool.Fori(1, PAIRS - 1) as i:
                    ffn_pair(ffn[l], i)
                share_lo(pool, nc.gpsimd.tensor_tensor, U_FFN[l] + 3 * PAIRS - 1, 1, first=False)

            inverse_root(0)
            ffn_all(0)
            inverse_root(1)
            with pool.Fori(0, RH) as h:
                pool.wait_ge(gvar_ready, h + 1)
                nc.gpsimd.tensor_tensor(rstd[:], veps[:], mhalf[:], ALU.pow).then_inc(grstd_ready, 1)
                pool.wait_ge(ro_hi, h + 1)
                nc.gpsimd.tensor_tensor(ol[:, bass.ds(4 * h, 4), :], ygn[:],
                                        oh[:, bass.ds(4 * h, 4), :].bitcast(F32),
                                        ALU.subtract).then_inc(ro_lo, 1)
            inverse_root(2)
            ffn_all(1)
            inverse_root(3)

        @block.scalar
        def _(act):
            def turned_hi(n, tr, *tiles):
                for m in tiles or range(TT):
                    for g in range(2):
                        act.wait_ge(xt_turned, 4 * n + 2 * m + g + 1)
                        nc.scalar.activation(
                            xh[:, 4 * g:4 * g + 4, m * P:(m + 1) * P],
                            ps[:, tr[m][g], :].rearrange("p (k n) -> p k n", k=4), ACT.Copy
                        ).then_inc(xh_ready, 1)

            def variance(n, m):
                act.wait_ge(mean_ready, TT * n + m + 1)
                if n or m:
                    act.wait_ge(var_ready, TT * n + m)
                nc.scalar.activation(squares, xtok[:, m, :], ACT.Square, bias=nmean[:, m:m + 1],
                                     accum_out=var[:, m:m + 1]).then_inc(var_ready, 1)

            def q_copy(t):
                act.wait_ge(used, RING * t + 1)
                if not isinstance(t, int) or t > 0:
                    act.wait_ge(s_ready, 4 * t)
                nc.scalar.activation(qT[:], halves(0), ACT.Copy, scale=HD ** -0.5).then_inc(q_copied, 1)

            def k_copy(t):
                act.wait_ge(used, RING * t + 2)
                nc.scalar.activation(kT[:], halves(1), ACT.Copy).then_inc(k_copied, 1)

            def exps(t, h):
                act.wait_ge(max_ready, 4 * t + h + 1)
                for m, (a, b) in enumerate(((0, P), (P, CAUSAL))):
                    last = nc.scalar.activation(sc[:, h % 2, a:b], sc[:, h % 2, a:b], ACT.Exp,
                                                bias=nmax[:, h, m:m + 1], accum_out=rsum[:, h, m:m + 1])
                last.then_inc(exp_ready, 1)

            def pt_copy(t, h):
                act.wait_ge(p_turned, 4 * t + h + 1)
                if h >= 2:
                    act.wait_ge(pv_done, 4 * t + h - 1)
                nc.scalar.activation(pt[:, h % 2, :], ps[:, 5 + h % 2, 0:CAUSAL], ACT.Copy)\
                    .then_inc(pt_ready, 1)

            def out_hi(t, pair):
                act.wait_ge(pv_done, 4 * t + 2 * pair + 2)
                nc.scalar.activation(oh[:, bass.ds(2 * t + pair, 1), :], halves(7)[:, pair:pair + 1, :],
                                     ACT.Copy).then_inc(o_hi, 1)

            def quad(t, core, copies):
                split_hi(act, U_ATT + 2, t)
                exps(core, 0)
                exps(core, 1)
                pt_copy(core, 0)
                pt_copy(core, 1)
                split_hi(act, U_ATT + 3, t)
                exps(core, 2)
                exps(core, 3)
                out_hi(core, 0)
                if copies:
                    q_copy(t)
                if copies:
                    split_hi(act, U_ATT + 4, t)
                    k_copy(t)
                pt_copy(core, 2)
                pt_copy(core, 3)
                out_hi(core, 1)
                if not copies:
                    split_hi(act, U_ATT + 4, t)

            turned_hi(0, TR_IN, 0)
            for i in range(2):
                act.wait_ge(first_loaded[i], 16)
                half = slice(i * UNIT // 2, (i + 1) * UNIT // 2)
                ins = nc.scalar.activation(whi[:, 0, half], raw[:, 0, half], ACT.Copy)
                ins.then_inc(hi_done if i else first_hi, 1)
                if i == 0:
                    turned_hi(0, TR_IN, 1)
            split_hi(act, 1)
            split_hi(act, 2)
            split_hi(act, 3)
            q_copy(0)
            split_hi(act, 4)
            k_copy(0)
            act.wait_ge(par_turned, 1)
            nc.scalar.activation(par[:], ps[:, 7, 0:par.shape[1]], ACT.Copy).then_inc(par_copied, 1)
            with act.Fori(1, QUADS) as t:
                quad(t, t - 1, True)
            quad(QUADS, QUADS - 1, False)
            variance(0, 0)
            split_hi(act, U_ATT_OUT + 5)
            variance(0, 1)
            turned_hi(1, TR_ATT)

            def conv_tap(l, i, part, u, s):
                if part == 1 and isinstance(i, int) and (i, s) == (PAIRS - 1, 0):
                    act.wait_ge(ffn[l]["last_gate"], 1)
                else:
                    act.wait_ge(used, up_unit(l, i, part) + RING * i + 1)
                at = part * (FT // 2) + 2 * i + s
                nc.scalar.activation(u[:, s, :], up_bank(part, s), ACT.Identity,
                                     bias=par[:, bass.ds(tap(l, 3) + at, 1)],
                                     scale=par[:, bass.ds(tap(l, 2) + at, 1)]).then_inc(ffn[l]["scaled"], 1)

            def ffn_conv(l, i, part, u):
                f = ffn[l]
                if not isinstance(i, int) or i > 0:
                    act.wait_ge(f["gelu_done"] if part == 0 else f["mult_done"], i)
                if isinstance(i, int) and i == 0 and l == 0 and part == 0:
                    act.wait_ge(par_copied, 1)
                for s in range(2):
                    conv_tap(l, i, part, u, s)

            def gelu(l, i):
                f = ffn[l]
                act.wait_ge(f["taps_done"], 2 * i + 1)
                if not isinstance(i, int) or i > 0:
                    act.wait_ge(f["mult_done"], i)
                nc.scalar.activation(ga[:], ua[:], ACT.Gelu).then_inc(f["gelu_done"], 1)

            def z_hi(l, i):
                f = ffn[l]
                act.wait_ge(f["mult_done"], i + 1)
                act.wait_ge(used, U_FFN[l] + 2 + RING * i)
                nc.scalar.activation(zh[:, 0], zf[:], ACT.Copy).then_inc(f["zh_done"], 1)

            def ffn_iter(l, i):
                u = U_FFN[l]
                z_hi(l, i - 1)
                split_hi(act, u + 1, i)
                ffn_conv(l, i, 0, ua)
                split_hi(act, u + 2, i)
                gelu(l, i)

            def ffn_all(l):
                split_hi(act, U_FFN[l] + 2)
                ffn_conv(l, 0, 0, ua)
                split_hi(act, U_FFN[l] + 3)
                gelu(l, 0)
                ffn_conv(l, 0, 1, ug)
                with act.Fori(1, PAIRS - 1) as i:
                    ffn_iter(l, i)
                    ffn_conv(l, i, 1, ug)
                    split_hi(act, U_FFN[l] + 3, i)
                ffn_iter(l, PAIRS - 1)
                f = ffn[l]
                act.wait_ge(f["mult_done"], PAIRS - 1)
                for s in range(2):
                    conv_tap(l, PAIRS - 1, 1, ug, s)
                    if s == 1:
                        split_hi(act, U_FFN[l] + 3 * PAIRS)
                    act.wait_ge(f["mult_done"], PAIRS + s)
                    nc.scalar.activation(zh[:, 1, s], zf[:, s], ACT.Copy).then_inc(f["zh_done"], 1)

            ffn_all(0)
            variance(1, 0)
            split_hi(act, U_RET + 1)
            turned_hi(2, TR_FFN, 0)
            split_hi(act, U_RET + 2)
            variance(1, 1)
            turned_hi(2, TR_FFN, 1)

            def ret_gain(h, banks):
                act.wait_ge(on_turned, h + 1)
                act.wait_ge(ro_lo, h + 1)
                for j in range(4):
                    nc.scalar.activation(ygn[:, j, :], halves(banks[j // 2])[:, j % 2, :], ACT.Identity,
                                         bias=par[:, bass.ds(4 * h + (GN + 2 * KD + j), 1)],
                                         scale=par[:, bass.ds(4 * h + (GN + j), 1)]).then_inc(y_ready, 1)

            def ret_hi(h):
                act.wait_ge(gated, h + 1)
                nc.scalar.activation(oh[:, bass.ds(4 * h, 4), :], ygn[:], ACT.Copy).then_inc(ro_hi, 1)

            def ret_head(h, before):
                if before:
                    split_hi(act, U_RET + 2, 2 * h)
                split_hi(act, U_RET + 3, 2 * h)
                if before:
                    ret_gain(h - 1, (4, 5))
                act.wait_ge(used, U_RET + 6 * h + 2)
                nc.scalar.activation(vt[:, 0, :], ps[:, 2, :], ACT.Copy).then_inc(rv_copied[0], 1)
                if before:
                    ret_hi(h - 1)
                split_hi(act, U_RET + 4, 2 * h)
                act.wait_ge(used, U_RET + 6 * h + 3)
                nc.scalar.activation(qT[:], halves(0), ACT.Copy).then_inc(rq_copied, 1)
                split_hi(act, U_RET + 5, 2 * h)
                act.wait_ge(used, U_RET + 6 * h + 4)
                nc.scalar.activation(kT[:], halves(1), ACT.Copy).then_inc(rk_copied, 1)
                split_hi(act, U_RET + 6, 2 * h)
                act.wait_ge(used, U_RET + 6 * h + 5)
                nc.scalar.activation(sg[:, 0:2, :], halves(4), ACT.Silu).then_inc(silu_done, 1)
                split_hi(act, U_RET + 7, 2 * h)
                act.wait_ge(used, U_RET + 6 * h + 6)
                nc.scalar.activation(sg[:, 2:4, :], halves(5), ACT.Silu).then_inc(silu_done, 1)

            ret_head(0, False)
            with act.Fori(1, RH) as h:
                ret_head(h, True)
            split_hi(act, U_RET_OUT + 2)
            split_hi(act, U_RET_OUT + 3)
            ret_gain(RH - 1, (2, 3))
            split_hi(act, U_RET_OUT + 4)
            ret_hi(RH - 1)
            for j in range(5, 9):
                split_hi(act, U_RET_OUT + j)
            variance(2, 0)
            split_hi(act, U_RET_OUT + 9)
            variance(2, 1)
            turned_hi(3, TR_RET)
            ffn_all(1)
            variance(3, 0)
            variance(3, 1)

        @block.vector
        def _(dve):
            def turned_lo(n, tr, *tiles):
                for m in tiles or range(TT):
                    for g in range(2):
                        dve.wait_ge(xh_ready, 4 * n + 2 * m + g + 1)
                        ks, ts = slice(4 * g, 4 * g + 4), slice(m * P, (m + 1) * P)
                        nc.vector.tensor_tensor(
                            xl[:, ks, ts], ps[:, tr[m][g], :].rearrange("p (k n) -> p k n", k=4),
                            xh[:, ks, ts].bitcast(F32), ALU.subtract).then_inc(xl_ready, 1)

            steps = [0]

            def step(ins):
                steps[0] += 1
                ins.then_inc(dve_ln, 1)

            def settle():
                dve.wait_ge(dve_ln, steps[0])

            def residual(n, m, acc):
                dve.wait_ge(acc_ready, 2 * n + m + 1)
                for c in range(2):
                    if (m, c) == (1, 1):
                        dve.wait_ge(used, LAST_UNIT[n] + 1)
                    half = xtok[:, m, c * BANK:(c + 1) * BANK]
                    step(nc.vector.scalar_tensor_tensor(out=half, in0=half, scalar=ALPHA,
                                                        in1=ps[:, acc[m][c], :], op0=ALU.mult, op1=ALU.add,
                                                        accum_out=half_sum[:, m, c:c + 1]))
                settle()
                nc.vector.tensor_scalar(nmean[:, m:m + 1], half_sum[:, m, 0:1], half_sum[:, m, 1:2],
                                        -1.0 / D, ALU.add, ALU.mult).then_inc(mean_ready, 1)

            def centre(n, m):
                if m == 0:
                    dve.wait_ge(lnp_loaded[n], 32)
                dve.wait_ge(mean_ready, TT * n + m + 1)
                step(nc.vector.scalar_tensor_tensor(out=lnt[:, m, :], in0=xtok[:, m, :],
                                                    scalar=nmean[:, m:m + 1], in1=lnp[:, n % 2, 0, :],
                                                    op0=ALU.add, op1=ALU.mult))
                dve.wait_ge(var_ready, TT * n + m + 1)
                nc.vector.tensor_scalar(veps[:, m:m + 1], var[:, m:m + 1], 1.0 / D, LN_EPS, ALU.mult, ALU.add)\
                    .then_inc(veps_ready, 1)

            def normal(n, m):
                settle()
                dve.wait_ge(rstd_ready, TT * n + m + 1)
                for c in range(2):
                    b = slice(c * BANK, (c + 1) * BANK)
                    nc.vector.scalar_tensor_tensor(out=xtok[:, m, b], in0=lnt[:, m, b],
                                                   scalar=rstd[:, m:m + 1], in1=lnp[:, n % 2, 1, b],
                                                   op0=ALU.mult, op1=ALU.add).then_inc(x_ready, 1)

            def layer_norm(n, acc):
                for m in range(TT):
                    residual(n, m, acc)
                    centre(n, m)
                    normal(n, m)

            def scores(t, h):
                g = 4 * t + h
                dve.wait_ge(s_ready, g + 1)
                if h >= 2:
                    dve.wait_ge(p_turned, g - 1)
                nc.vector.scalar_tensor_tensor(out=sc[:, h % 2, :], in0=dist[:], scalar=slopes[:, bass.ds(g, 1)],
                                               in1=ps[:, score_bank(t, h), 0:CAUSAL], op0=ALU.mult,
                                               op1=ALU.add).then_inc(biased, 1)
                dve.wait_ge(biased, g + 1)
                for m, (a, b) in enumerate(((0, P), (P, CAUSAL))):
                    last = nc.vector.tensor_reduce(nmax[:, h, m:m + 1], sc[:, h % 2, a:b], AX_X, ALU.max,
                                                   negate=True)
                last.then_inc(max_ready, 1)

            def normalise(t, h):
                g = 4 * t + h
                dve.wait_ge(exp_ready, g + 1)
                nc.vector.reciprocal(rinv[:, h, :], rsum[:, h, :]).then_inc(inv_ready, 1)
                dve.wait_ge(inv_ready, g + 1)
                for m, (a, b) in enumerate(((0, P), (P, CAUSAL))):
                    last = nc.vector.tensor_scalar(sc[:, h % 2, a:b], sc[:, h % 2, a:b], rinv[:, h, m:m + 1],
                                                   None, ALU.mult)
                last.then_inc(p_ready, 1)

            def out_lo(t, pair):
                dve.wait_ge(o_hi, 2 * t + pair + 1)
                at = bass.ds(2 * t + pair, 1)
                nc.vector.tensor_tensor(ol[:, at, :], halves(7)[:, pair:pair + 1, :],
                                        oh[:, at, :].bitcast(F32), ALU.subtract).then_inc(o_lo, 1)

            def v_copy(t):
                dve.wait_ge(used, RING * t + 3)
                if not isinstance(t, int) or t > 0:
                    dve.wait_ge(pv_done, 4 * t)
                nc.vector.tensor_copy(vt[:, :, 0:HALF], halves(2)).then_inc(v_copied, 1)

            def quad(t, core, copies):
                scores(core, 0)
                scores(core, 1)
                normalise(core, 0)
                normalise(core, 1)
                split_lo(dve, U_ATT + 2, t)
                scores(core, 2)
                scores(core, 3)
                split_lo(dve, U_ATT + 3, t)
                normalise(core, 2)
                normalise(core, 3)
                out_lo(core, 0)
                if copies:
                    split_lo(dve, U_ATT + 4, t)
                out_lo(core, 1)
                if not copies:
                    split_lo(dve, U_ATT + 4, t)
                if copies:
                    v_copy(t)

            nc.vector.memset(st6[:], 0.0).then_inc(o_lo, 1)
            nc.vector.memset(var[:], 0.0).then_inc(ro_lo, 1)
            turned_lo(0, TR_IN, 0)
            for i in range(2):
                dve.wait_ge(hi_done if i else first_hi, 1)
                half = slice(i * UNIT // 2, (i + 1) * UNIT // 2)
                nc.vector.tensor_tensor(wlo[:, 0, half], raw[:, 0, half], whi[:, 0, half].bitcast(F32),
                                        ALU.subtract).then_inc(lo_done if i else first_lo, 1)
                if i == 0:
                    turned_lo(0, TR_IN, 1)
            split_lo(dve, 1)
            split_lo(dve, 2)
            split_lo(dve, 3)
            split_lo(dve, 4)
            v_copy(0)
            dve.wait_ge(const_step, consts["attention"])
            with dve.Fori(1, QUADS) as t:
                quad(t, t - 1, True)
            quad(QUADS, QUADS - 1, False)
            layer_norm(0, ACC_ATT)
            turned_lo(1, TR_ATT)
            split_lo(dve, U_ATT_OUT + 5)

            def conv_tap(l, i, part, u, s, back):
                f = ffn[l]
                if back == 1:
                    dve.wait_ge(f["scaled"], 4 * i + 2 * part + s + 1)
                else:
                    dve.wait_ge(f["tap1"], 4 * i + 2 * part + s + 1)
                at = part * (FT // 2) + 2 * i + s
                ins = nc.vector.scalar_tensor_tensor(
                    out=u[:, s, back:SEQ], in0=up_bank(part, s)[:, 0:SEQ - back],
                    scalar=par[:, bass.ds(tap(l, 2 - back) + at, 1)], in1=u[:, s, back:SEQ],
                    op0=ALU.mult, op1=ALU.add)
                if back == 1:
                    ins.then_inc(f["tap1"], 1)
                return ins

            def ffn_taps(l, i, part, u):
                for back in (1, 2):
                    for s in range(2):
                        last = conv_tap(l, i, part, u, s, back)
                last.then_inc(ffn[l]["taps_done"], 1)

            def ffn_iter(l, i):
                u = U_FFN[l]
                split_lo(dve, u + 1, i)
                ffn_taps(l, i, 0, ua)

            def ffn_all(l):
                split_lo(dve, U_FFN[l] + 2)
                ffn_taps(l, 0, 0, ua)
                split_lo(dve, U_FFN[l] + 3)
                ffn_taps(l, 0, 1, ug)
                with dve.Fori(1, PAIRS - 1) as i:
                    ffn_iter(l, i)
                    split_lo(dve, U_FFN[l] + 2, i)
                    ffn_taps(l, i, 1, ug)
                    split_lo(dve, U_FFN[l] + 3, i)
                ffn_iter(l, PAIRS - 1)
                share_lo(dve, nc.vector.tensor_tensor, U_FFN[l] + 3 * PAIRS - 1, 0, first=True)
                f = ffn[l]
                for s in range(2):
                    conv_tap(l, PAIRS - 1, 1, ug, s, 1)
                    conv_tap(l, PAIRS - 1, 1, ug, s, 2).then_inc(f["last_taps"], 1)
                    if s == 0:
                        dve.wait_ge(f["gelu_done"], PAIRS)
                        dve.wait_ge(f["zh_done"], PAIRS - 1)
                        dve.wait_ge(f["z_ready"], PAIRS - 1)
                    dve.wait_ge(f["last_taps"], s + 1)
                    nc.vector.tensor_tensor(zf[:, s], ga[:, s], ug[:, s], ALU.mult).then_inc(f["mult_done"], 1)
                    dve.wait_ge(f["zh_done"], PAIRS + s)
                    nc.vector.tensor_tensor(zl[:, 1, s], zf[:, s], zh[:, 1, s].bitcast(F32),
                                            ALU.subtract).then_inc(f["z_ready"], 1)
                dve.wait_ge(lo_done, U_FFN[l] + 3 * PAIRS)
                split_lo(dve, U_FFN[l] + 3 * PAIRS)

            ffn_all(0)
            residual(1, 0, ACC_FFN)
            centre(1, 0)
            normal(1, 0)
            residual(1, 1, ACC_FFN)
            turned_lo(2, TR_FFN, 0)
            share_lo(dve, nc.vector.tensor_tensor, U_RET + 1, 1, first=False)
            centre(1, 1)
            normal(1, 1)
            turned_lo(2, TR_FFN, 1)

            GN_STEPS = TT + 2
            dve.wait_ge(const_step, consts["retention"])
            def ret_gate(h):
                dve.wait_ge(y_ready, 4 * h + 4)
                dve.wait_ge(silu_done, 2 * h + 2)
                nc.vector.tensor_tensor(ygn[:], ygn[:], sg[:], ALU.mult).then_inc(gated, 1)

            def ret_head(h, before):
                split_lo(dve, U_RET + 2, 2 * h)
                split_lo(dve, U_RET + 3, 2 * h)
                if before:
                    ret_gate(h - 1)
                dve.wait_ge(used, U_RET + 6 * h + 2)
                nc.vector.tensor_copy(vt[:, 1, :], ps[:, 3, :]).then_inc(rv_copied[1], 1)
                for j in range(4, 7):
                    split_lo(dve, U_RET + j, 2 * h)
                dve.wait_ge(rs_ready, h + 1)
                nc.vector.tensor_tensor(pt[:, 0:1, :], ps[:, 6:7, 0:CAUSAL], decay[:, bass.ds(h, 1), :],
                                        ALU.mult).then_inc(decayed, 1)
                split_lo(dve, U_RET + 7, 2 * h)
                for m, bank in enumerate((7, 0)):
                    dve.wait_ge(ro_ready, TT * h + m + 1)
                    nc.vector.bn_stats(st6[:, m, 0, :], ps[:, bank, :]).then_inc(dve_gn, 1)
                st = [st6[:, :, 0, i] for i in range(6)]
                dve.wait_ge(dve_gn, GN_STEPS * h + TT)
                nc.vector.tensor_tensor(gm[:, 0, :], st[1], st[4], ALU.add)
                nc.vector.tensor_tensor(gm[:, 1, :], st[1], st[4], ALU.subtract)
                nc.vector.tensor_tensor(gm[:, 2, :], st[2], st[5], ALU.add).then_inc(dve_gn, 1)
                dve.wait_ge(dve_gn, GN_STEPS * h + TT + 1)
                nc.vector.tensor_scalar(gmean[:], gm[:, 0, :], 0.5, None, ALU.mult)
                nc.vector.scalar_tensor_tensor(out=gm[:, 3, :], in0=gm[:, 1, :], scalar=0.25, in1=gm[:, 1, :],
                                               op0=ALU.mult, op1=ALU.mult)
                nc.vector.tensor_scalar(gm[:, 4, :], gm[:, 2, :], 1.0 / RV, GN_EPS, ALU.mult, ALU.add)\
                    .then_inc(dve_gn, 1)
                dve.wait_ge(dve_gn, GN_STEPS * h + TT + 2)
                nc.vector.tensor_tensor(veps[:], gm[:, 3, :], gm[:, 4, :], ALU.add).then_inc(gvar_ready, 1)
                dve.wait_ge(grstd_ready, h + 1)
                for m, bank in enumerate((7, 0)):
                    nc.vector.tensor_scalar(onrm[:, m, :], ps[:, bank, :], gmean[:, m:m + 1], rstd[:, m:m + 1],
                                            ALU.subtract, ALU.mult).then_inc(on_ready, 1)

            ret_head(0, False)
            with dve.Fori(1, RH) as h:
                ret_head(h, True)
            split_lo(dve, U_RET_OUT + 2)
            split_lo(dve, U_RET_OUT + 3)
            ret_gate(RH - 1)
            for j in range(4, 9):
                split_lo(dve, U_RET_OUT + j)
            layer_norm(2, ACC_RET)
            turned_lo(3, TR_RET)
            split_lo(dve, U_RET_OUT + 9)
            ffn_all(1)
            layer_norm(3, ACC_FFN)

        @block.tensor
        def _(pe):
            def turn_x(m, tr, n=None):
                for g in range(2):
                    if n is not None:
                        pe.wait_ge(x_ready, 4 * n + 2 * m + g + 1)
                    for k in range(4):
                        last = nc.tensor.transpose(ps[:, tr[m][g], k * P:(k + 1) * P],
                                                   xtok[:, m, (4 * g + k) * P:(4 * g + k + 1) * P], ident[:])
                    last.then_inc(xt_turned, 1)

            def last_unit(product):
                for n in range(2):
                    for kk in range(2):
                        last = product(kk, n)
                    last.then_inc(used if n else acc_ready, 1)

            def turn_after_ln(n, tr):
                for m in range(TT):
                    turn_x(m, tr, n)

            def x_parts(n, m, g):
                pe.wait_ge(xl_ready, 4 * (n + 1) + 2 * m + g + 1)

            def project_chunk(t, x_):
                u, j, half = x_ // 4, x_ // 2 % 2, x_ % 2
                if isinstance(t, int) and x_ < 2:
                    x_parts(-1, 1, x_)
                if isinstance(t, int) and x_ == 0:
                    pe.wait_ge(first_lo, 1)
                elif x_ % 4 == 0 or isinstance(t, int) and x_ == 1:
                    unit_ready(pe, U_ATT + u, t)
                    if not isinstance(t, int) or t > 0:
                        pe.wait_ge((q_copied, k_copied, v_copied)[u], t)
                ks = range(4 * half, 4 * half + 4)
                if u < 2:
                    last = feature_tile(halves(u)[:, j, :], u, j, ks)
                else:
                    h, l = cols(whi, u), cols(wlo, u)
                    for k in ks:
                        last = products(halves(2)[:, j, :], xh[:, k, j * P:(j + 1) * P],
                                        xl[:, k, j * P:(j + 1) * P], h[:, k, :], l[:, k, :],
                                        k == 0, k == KD - 1)
                if x_ % 4 == 3:
                    last.then_inc(used, 1)

            def head_rows(h):
                return slice(HD * (h % 2), HD * (h % 2) + HD), h // 2

            def score(t, h):
                rs, pair = head_rows(h)
                if h == 0:
                    pe.wait_ge(q_copied, t + 1)
                    pe.wait_ge(k_copied, t + 1)
                if h >= 2:
                    pe.wait_ge(biased, 4 * t + h - 1)
                if isinstance(t, int) and t == QUADS - 1 and h == 3:
                    pe.wait_ge(pt_ready, 4 * t + 1)
                bank = ps[:, score_bank(t, h), :]
                nc.tensor.matmul(bank[:, 0:P], qT[rs, pair, 0:P], kT[rs, pair, 0:P], start=True, stop=True)
                nc.tensor.matmul(bank[:, P:CAUSAL], qT[rs, pair, P:SEQ], kT[rs, pair, :],
                                 start=True, stop=True).then_inc(s_ready, 1)

            def turn_p(t, h):
                pe.wait_ge(p_ready, 4 * t + h + 1)
                for b in range(3):
                    last = nc.tensor.transpose(ps[:, 5 + h % 2, b * P:(b + 1) * P],
                                               sc[:, h % 2, b * P:(b + 1) * P], ident[:])
                last.then_inc(p_turned, 1)

            def values(t, pair):
                hs = (2 * pair, 2 * pair + 1)
                if pair == 0:
                    pe.wait_ge(v_copied, t + 1)
                    pe.wait_ge(par_copied, 1)
                pe.wait_ge(o_lo, 2 * t + pair + 1)
                for h in hs:
                    pe.wait_ge(pt_ready, 4 * t + h + 1)
                    nc.tensor.matmul(halves(7)[head_rows(h)[0], pair, :], vt[:, 0, h * HD:(h + 1) * HD],
                                     pt[:, h % 2, 0:SEQ], start=True, stop=False)
                for h in hs:
                    nc.tensor.matmul(halves(7)[head_rows(h)[0], pair, P:SEQ], vt[:, 1, h * HD:(h + 1) * HD],
                                     pt[:, h % 2, SEQ:CAUSAL], start=False, stop=True).then_inc(pv_done, 1)

            def core(t, x_, last=False):
                at_score, at_turn, at_values = ((0, 4), (3, 7), (5, 9)) if last else ((0, 5), (4, 9), (6, 11))
                for pair in range(2):
                    if x_ == at_score[pair]:
                        score(t, 2 * pair)
                        score(t, 2 * pair + 1)
                    if x_ == at_turn[pair]:
                        turn_p(t, 2 * pair)
                        turn_p(t, 2 * pair + 1)
                    if x_ == at_values[pair]:
                        values(t, pair)

            pe.wait_ge(const_step, 2)
            for m in range(TT):
                pe.wait_ge(x_loaded[m], 16)
                turn_x(m, TR_IN)
            for x_ in range(12):
                project_chunk(0, x_)
            pe.wait_ge(par_loaded, 16 * 6)
            for i in range(8):
                nc.tensor.transpose(ps[:, 7, i * FT:(i + 1) * FT], stage[:, i, :], ident[0:FT, 0:FT])
            for i in range(2):
                last = nc.tensor.transpose(ps[:, 7, GN + i * 2 * KD:GN + (i + 1) * 2 * KD], gstage[:, i, :],
                                           ident[0:2 * KD, 0:2 * KD])
            last.then_inc(par_turned, 1)
            with pe.Fori(1, QUADS) as t:
                for x_ in range(12):
                    core(t - 1, x_)
                    project_chunk(t, x_)
            def att_out(j, m, kk, columns=range(2)):
                k = 2 * j + kk
                return out_rows(ACC_ATT, oh[:, k, :], ol[:, k, :], U_ATT_OUT + j, m, kk, k == 0,
                                k == KD - 1, columns)

            order = [(j, m, kk) for j in range(2) for m in range(TT) for kk in range(2)]
            order += [(j, m, kk) for m in range(TT) for j in (2, 3) for kk in range(2)]
            for x_, (j, m, kk) in enumerate(order[:-2]):
                core(QUADS - 1, x_, last=True)
                if x_ == 2:
                    pe.wait_ge(v_copied, QUADS)
                if (m, kk) == (0, 0):
                    unit_ready(pe, U_ATT_OUT + j)
                    pe.wait_ge(o_lo, 1 + 2 * (QUADS - 1) if j < 3 else 1 + 2 * QUADS)
                last = att_out(j, m, kk)
                if (j, m, kk) == (3, 0, 1):
                    last.then_inc(acc_ready, 1)
                if (m, kk) == (1, 1):
                    last.then_inc(used, 1)
            last_unit(lambda kk, n: att_out(3, 1, kk, [n]))
            turn_after_ln(0, TR_ATT)

            def first_tile(dst, c, j, after_ln):
                h, l = cols(whi, c % RING), cols(wlo, c % RING)
                for n, (w, x_, ready) in enumerate(((h, xh, xh_ready), (l, xh, xh_ready), (h, xl, xl_ready))):
                    for k in range(KD):
                        if n != 1 and k % 4 == 0:
                            pe.wait_ge(ready, 4 * (after_ln + 1) + 2 + k // 4 + 1)
                        nc.tensor.matmul(dst, w[:, k, j * P:(j + 1) * P], x_[:, k, :],
                                         start=n == 0 and k == 0, stop=n == 2 and k == KD - 1)

            def up_pair(l, i, part, after_ln=None):
                c = up_unit(l, i, part)
                unit_ready(pe, c, i)
                if not isinstance(i, int) or i > 0:
                    pe.wait_ge(ffn[l]["taps_done"], 2 * i + part - 1)
                if after_ln is None:
                    last = feature_tile(up_bank(part, 0), c, 0)
                else:
                    first_tile(up_bank(part, 0), c, 0, after_ln)
                if part == 1 and isinstance(i, int) and i == PAIRS - 1:
                    last.then_inc(ffn[l]["last_gate"], 1)
                feature_tile(up_bank(part, 1), c, 1).then_inc(used, 1)

            def down(l, c, m, kk, z=0, first=False, last=False, columns=range(2)):
                return out_rows(ACC_FFN, zh[:, z, kk, :], zl[:, z, kk, :], c, m, kk,
                                first and kk == 0, last and kk == 1, columns)

            def down_pair(l, i, first=False):
                c = U_FFN[l] + 1
                unit_ready(pe, c, i)
                pe.wait_ge(ffn[l]["z_ready"], i)
                for m in range(TT):
                    for kk in range(2):
                        ins = down(l, c, m, kk, first=first)
                ins.then_inc(used, 1)

            def ffn_all(l, after_ln):
                up_pair(l, 0, 0, after_ln)
                up_pair(l, 0, 1)
                up_pair(l, 1, 0)
                up_pair(l, 1, 1)
                down_pair(l, 1, first=True)
                with pe.Fori(2, PAIRS - 1) as i:
                    up_pair(l, i, 0)
                    up_pair(l, i, 1)
                    down_pair(l, i)
                up_pair(l, PAIRS - 1, 0)
                up_pair(l, PAIRS - 1, 1)
                cs = [U_FFN[l] + 3 * PAIRS - 2, U_FFN[l] + 3 * PAIRS - 1]
                for z, c in enumerate(cs):
                    for kk in range(2):
                        if (z, kk) == (1, 0):
                            pe.wait_ge(lo_half, 3 if l else 1)
                        else:
                            unit_ready(pe, c)
                        pe.wait_ge(ffn[l]["z_ready"], PAIRS + kk if z else PAIRS - 1)
                        last = down(l, c, 0, kk, z, last=z == 1)
                last.then_inc(acc_ready, 1)
                for kk in range(2):
                    last = down(l, cs[0], 1, kk)
                last.then_inc(used, 1)
                last_unit(lambda kk, n: down(l, cs[1], 1, kk, 1, last=True, columns=[n]))

            ffn_all(0, 0)

            def ret_v(h, j, tiles=range(TT), ks=range(4)):
                c = U_RET + j
                wh, wl = quarter(whi, c % RING), quarter(wlo, c % RING)
                for m in tiles:
                    for kk in ks:
                        k = 4 * j + kk
                        last = products(ps[:, 2 + m, :], xh[:, k, m * P:(m + 1) * P],
                                        xl[:, k, m * P:(m + 1) * P], wh[:, kk, :], wl[:, kk, :],
                                        k == 0, k == KD - 1)
                if m == 1:
                    last.then_inc(used, 1)

            def ret_turn(h, banks):
                for m in range(TT):
                    pe.wait_ge(on_ready, TT * h + m + 1)
                    for j in range(4):
                        last = nc.tensor.transpose(halves(banks[j // 2])[:, j % 2, m * P:(m + 1) * P],
                                                   onrm[:, m, j * P:(j + 1) * P], ident[:])
                last.then_inc(on_turned, 1)

            def ret_head(h):
                for j in range(2, 4):
                    c = U_RET + j
                    unit_ready(pe, c, 2 * h)
                    feature_tile(halves(j - 2)[:, 0, :], c, 0)
                    feature_tile(halves(j - 2)[:, 1, :], c, 1).then_inc(used, 1)
                c = U_RET + 4
                unit_ready(pe, c, 2 * h)
                feature_tile(halves(4)[:, 0, :], c, 0)
                pe.wait_ge(rq_copied, h + 1)
                pe.wait_ge(rk_copied, h + 1)
                for m, (a, b) in enumerate(((0, SEQ), (SEQ, CAUSAL))):
                    for k in range(2):
                        last = nc.tensor.matmul(ps[:, 6, a:b], kT[:, k, m * P:(m + 1) * P],
                                                qT[:, k, m * P:SEQ], start=k == 0, stop=k == 1)
                last.then_inc(rs_ready, 1)
                feature_tile(halves(4)[:, 1, :], c, 1).then_inc(used, 1)
                unit_ready(pe, c + 1, 2 * h)
                feature_tile(halves(5)[:, 0, :], c + 1, 0)
                pe.wait_ge(decayed, h + 1)
                pe.wait_ge(rv_copied[0], h + 1)
                pe.wait_ge(rv_copied[1], h + 1)
                nc.tensor.matmul(ps[:, 7, :], pt[:, 0, 0:P], vt[:, 0, :], start=True, stop=True)\
                    .then_inc(ro_ready, 1)
                nc.tensor.matmul(ps[:, 0, :], pt[:, 0, P:SEQ], vt[:, 0, :], start=True, stop=False)
                nc.tensor.matmul(ps[:, 0, :], pt[:, 0, SEQ:CAUSAL], vt[:, 1, :], start=False, stop=True)\
                    .then_inc(ro_ready, 1)
                feature_tile(halves(5)[:, 1, :], c + 1, 1).then_inc(used, 1)

            turn_x(0, TR_FFN, 1)
            for j in range(2):
                unit_ready(pe, U_RET + j)
                x_parts(1, 0, j)
                ret_v(0, j, [0], range(2 if j else 4))
            turn_x(1, TR_FFN, 1)
            ret_v(0, 1, [0], range(2, 4))
            for j in range(2):
                x_parts(1, 1, j)
                ret_v(0, j, [1])
            ret_head(0)
            with pe.Fori(1, RH) as h:
                unit_ready(pe, U_RET, 2 * h)
                ret_v(h, 0)
                pe.wait_ge(silu_done, 2 * h)
                ret_turn(h - 1, (4, 5))
                unit_ready(pe, U_RET + 1, 2 * h)
                ret_v(h, 1)
                ret_head(h)

            def ret_out(j, m, kk, columns=range(2)):
                k = 2 * j + kk
                return out_rows(ACC_RET, oh[:, k, :], ol[:, k, :], U_RET_OUT + j, m, kk, k == 0,
                                k == 2 * KD - 1, columns)

            order = [(j, m, kk) for j in range(6) for m in range(TT) for kk in range(2)]
            order += [(j, m, kk) for m in range(TT) for j in range(6, 8) for kk in range(2)]
            for j, m, kk in order[:-2]:
                if (j, m, kk) == (0, 1, 0):
                    pe.wait_ge(silu_done, 2 * RH)
                if (m, kk) == (0, 0):
                    if j == 2:
                        ret_turn(RH - 1, (2, 3))
                    unit_ready(pe, U_RET_OUT + j)
                    pe.wait_ge(ro_lo, j // 2 + 2)
                last = ret_out(j, m, kk)
                if (j, m, kk) == (7, 0, 1):
                    last.then_inc(acc_ready, 1)
                if (m, kk) == (1, 1):
                    last.then_inc(used, 1)
            last_unit(lambda kk, n: ret_out(7, 1, kk, [n]))
            turn_after_ln(2, TR_RET)
            ffn_all(1, 2)


_INS = ["x", "att_w_in", "att_w_out", "ret_w_in", "ret_w_out", "ret_gn_g", "ret_gn_b", "mix_ln_g",
        "mix_ln_b", "ffn_ln_g", "ffn_ln_b", "ffn_w_up", "ffn_conv_w", "ffn_conv_b", "ffn_w_down"]
_OUTS = [((1, SEQ, D), "float32")]


def kernel(**inputs):
    import numpy as _np
    import concourse.bacc as _bacc
    from concourse import mybir as _mybir
    from concourse.bass_utils import run_bass_kernel_spmd as _run

    nc = _bacc.Bacc("TRN2", target_bir_lowering=False, num_devices=1)
    arrays, args = {}, []
    for name in _INS:
        a = _np.ascontiguousarray(inputs[name])
        arrays[f"in_{name}_dram"] = a
        args.append(nc.dram_tensor(f"in_{name}_dram", a.shape, _mybir.dt.from_np(a.dtype), kind="ExternalInput").ap())
    for i, (shape, dtype) in enumerate(_OUTS):
        dt = _mybir.dt.from_np(_np.dtype(dtype))
        args.append(nc.dram_tensor(f"out_{i}_dram", shape, dt, kind="ExternalOutput").ap())
    decoder_trunk(nc, *args)
    r = _run(nc, [arrays], core_ids=[0])
    got = tuple(r.results[0][f"out_{i}_dram"] for i in range(len(_OUTS)))
    return got[0]
```

```python
from contextlib import ExitStack

import concourse.bass as bass
from concourse import mybir

F32 = mybir.dt.float32
F32R = mybir.dt.float32r
ALU = mybir.AluOpType
ACT = mybir.ActivationFunctionType
AX_X = mybir.AxisListType.X

P = 128
SEQ = 256
TT = SEQ // P
D = 1024
KD = D // P
HEADS = 16
HD = D // HEADS
QUADS = 4
RH = 4
RK = D // RH
RV = 2 * RK
FFN = 2816
FT = 2 * FFN // P
PAIRS = FFN // 256
UNIT = 2048
RING = 3
HALF = 256
BANK = 512
LN_EPS = 1e-5
GN_EPS = 1e-5
ALPHA = (2.0 * 2) ** 0.25
MASKED = -1e33
CAUSAL = P + SEQ

U_ATT = 0
U_ATT_OUT = U_ATT + 3 * QUADS
U_FFN = [U_ATT_OUT + 4, 0]
U_RET = U_FFN[0] + 3 * PAIRS
U_RET_OUT = U_RET + 6 * RH
U_FFN[1] = U_RET_OUT + 8
UNITS = U_FFN[1] + 3 * PAIRS
LAST_UNIT = [U_FFN[0] - 1, U_RET - 1, U_FFN[1] - 1, UNITS - 1]

ACC_ATT, TR_ATT = [[0, 1], [2, 4]], [[5, 6], [7, 3]]
ACC_FFN, TR_FFN = [[2, 3], [0, 1]], [[6, 7], [4, 5]]
ACC_RET, TR_RET = [[1, 6], [4, 5]], [[2, 3], [0, 7]]
TR_IN = [[0, 1], [2, 3]]

TILE_HALVES = [(0, 0), (0, 1), (1, 0), (1, 1)]

OUT_PIECES = [slice(a, b) for a, b in ((0, BANK), (BANK, D), (0, BANK), (BANK, D - HALF), (D - HALF, D))]

PIECES = [(0, 0, 2, False), (0, 2, 4, False), (0, 4, 8, True), (1, 0, 4, False), (1, 4, 8, True)]


def decoder_trunk(nc, x, att_w_in, att_w_out, ret_w_in, ret_w_out, ret_gn_g, ret_gn_b, mix_ln_g,
                  mix_ln_b, ffn_ln_g, ffn_ln_b, ffn_w_up, ffn_conv_w, ffn_conv_b, ffn_w_down, out):
    with ExitStack() as ctx:
        def sb(name, shape, dt=F32):
            return ctx.enter_context(nc.sbuf_tensor(name, shape, dt))

        def sem(name):
            return ctx.enter_context(nc.semaphore(name))

        raw = sb("raw", [P, RING, UNIT])
        whi = sb("whi", [P, RING, UNIT], F32R)
        wlo = sb("wlo", [P, RING, UNIT], F32R)
        xtok = sb("xtok", [P, TT, D])
        xh = sb("xh", [P, KD, SEQ], F32R)
        xl = sb("xl", [P, KD, SEQ], F32R)
        oh = sb("oh", [P, 2 * KD, SEQ], F32R)
        ol = sb("ol", [P, 2 * KD, SEQ], F32R)
        lnp = sb("lnp", [P, 2, 2, D])
        par = sb("par", [P, 8 * FT + 2 * 2 * KD])
        ident = sb("ident", [P, P])
        dist = sb("dist", [P, CAUSAL])
        slopes = sb("slopes", [P, HEADS])
        decay = sb("decay", [P, RH, CAUSAL])
        powers = sb("powers", [P, 32])
        gbase = sb("gbase", [P, 32])
        gpow = sb("gpow", [P, 32])
        gkey = sb("gkey", [P, 2])
        nkey = sb("nkey", [P, 1])
        mhalf = sb("mhalf", [P, TT])
        gm = sb("gm", [P, 5, TT])
        gmean = sb("gmean", [P, TT])
        st6 = sb("st6", [P, TT, 6])
        half_sum = sb("half_sum", [P, TT, 2])
        nmean = sb("nmean", [P, TT])
        var = sb("var", [P, TT])
        lnt = sb("lnt", [P, TT, D])
        stage = lnt[0:FT, 0, :].rearrange("f (w n) -> f w n", w=8)
        gstage = lnt[0:2 * KD, 1, 0:2 * P].rearrange("f (w n) -> f w n", w=2)
        veps = sb("veps", [P, TT])
        rstd = sb("rstd", [P, TT])
        qT = sb("qT", [P, 2, SEQ])
        kT = sb("kT", [P, 2, SEQ])
        vt = sb("vt", [P, TT, HALF])
        sc = sb("sc", [P, 2, CAUSAL])
        pt = sb("pt", [P, 2, CAUSAL])
        nmax = sb("nmax", [P, 4, TT])
        rsum = sb("rsum", [P, 4, TT])
        rinv = sb("rinv", [P, 4, TT])
        ua = sb("ua", [P, 2, SEQ])
        ug = sb("ug", [P, 2, SEQ])
        ga = sb("ga", [P, 2, SEQ])
        zf = sb("zf", [P, 2, SEQ])
        zh = sb("zh", [P, 2, 2, SEQ], F32R)
        zl = sb("zl", [P, 2, 2, SEQ], F32R)
        vh, vl = (t[:].rearrange("p a b n -> p a (b n)") for t in (zh, zl))
        sh = sb("sh", [P, CAUSAL], F32R)
        sl = sb("sl", [P, CAUSAL], F32R)
        onrm = sb("onrm", [P, TT, RV])
        squares = onrm[:, :, :].rearrange("p m n -> p (m n)")
        ygn = sb("ygn", [P, 4, SEQ])
        sg = sb("sg", [P, 4, SEQ])
        ps = ctx.enter_context(nc.psum_tensor("ps", [P, 8, BANK], F32))

        x_loaded = [sem(f"x_loaded{i}") for i in range(2 * TT)]
        piece_loaded = [sem(f"piece_loaded{i}") for i in range(len(PIECES))]
        piece_hi = sem("piece_hi")
        piece_lo = sem("piece_lo")
        par_loaded = sem("par_loaded")
        lnp_loaded = [sem(f"lnp_loaded{i}") for i in range(4)]
        loaded = [sem(f"loaded{i}") for i in range(RING)]
        hi_done = sem("hi_done")
        lo_done = sem("lo_done")
        lo_half = sem("lo_half")
        used = sem("used")
        stored = sem("stored")
        const_step = sem("const_step")
        par_turned = sem("par_turned")
        par_copied = sem("par_copied")
        acc_ready = sem("acc_ready")
        dve_ln = sem("dve_ln")
        mean_ready = sem("mean_ready")
        var_ready = sem("var_ready")
        veps_ready = sem("veps_ready")
        rstd_ready = sem("rstd_ready")
        x_ready = sem("x_ready")
        xt_turned = sem("xt_turned")
        xh_ready = sem("xh_ready")
        xl_ready = sem("xl_ready")
        q_copied = sem("q_copied")
        k_copied = sem("k_copied")
        v_copied = sem("v_copied")
        s_ready = sem("s_ready")
        biased = sem("biased")
        max_ready = sem("max_ready")
        exp_ready = sem("exp_ready")
        inv_ready = sem("inv_ready")
        p_ready = sem("p_ready")
        p_turned = sem("p_turned")
        pt_ready = sem("pt_ready")
        pv_done = sem("pv_done")
        o_hi = sem("o_hi")
        o_lo = sem("o_lo")
        rq_copied = sem("rq_copied")
        rk_copied = sem("rk_copied")
        rv_hi = sem("rv_hi")
        rv_lo = sem("rv_lo")
        rs_ready = sem("rs_ready")
        decayed = sem("decayed")
        decayed_hi = sem("decayed_hi")
        decayed_lo = sem("decayed_lo")
        ro_ready = sem("ro_ready")
        dve_gn = sem("dve_gn")
        gvar_ready = sem("gvar_ready")
        grstd_ready = sem("grstd_ready")
        on_ready = sem("on_ready")
        on_turned = sem("on_turned")
        y_ready = sem("y_ready")
        silu_done = sem("silu_done")
        gated = sem("gated")
        ro_hi = sem("ro_hi")
        ro_lo = sem("ro_lo")
        ffn = [{n: sem(f"{n}_{l}") for n in (
            "scaled", "tap1", "taps_done", "gelu_done", "mult_done", "zh_done", "z_ready",
            "last_gate", "last_taps")}
            for l in range(2)]

        def cols(t, slot):
            return t[:, slot].rearrange("p (k n) -> p k n", k=KD)

        def rows(t, slot):
            return t[:, slot].rearrange("p (k n) -> p k n", k=2)

        def quarter(t, slot):
            return t[:, slot].rearrange("p (k n) -> p k n", k=4)

        def halves(bank):
            return ps[:, bank, :].rearrange("p (j n) -> p j n", j=2)

        def apart(u, j):
            return ps[:, u + 4 * j, 0:SEQ]

        def up_bank(part, s):
            return ps[:, 4 + 2 * part + s, 0:SEQ]

        def tap(l, w):
            return (4 * l + w) * FT

        def up_unit(l, i, part):
            return U_FFN[l] + part if isinstance(i, int) and i == 0 else U_FFN[l] - 1 + part

        def score_bank(t, h):
            return (3, 5)[h % 2] if isinstance(t, int) and t == QUADS - 1 else 3 + h % 2

        GN = 8 * FT

        def load(sp, c, i, view, src):
            s = c % RING
            if not (isinstance(i, int) and c + RING * i < RING):
                sp.wait_ge(lo_done, c + RING * i - RING + 1)
            sp.dma_start(view(raw, s), src).then_inc(loaded[s], 16)

        def split_hi(act, c, i=0):
            if isinstance(i, int) and c + RING * i >= UNITS:
                return
            s = c % RING
            act.wait_ge(loaded[s], 16 * (c // RING + i + (s == 2)))
            if not (isinstance(i, int) and c + RING * i < RING):
                act.wait_ge(used, c + RING * i - RING + 1)
            nc.scalar.activation(whi[:, s], raw[:, s], ACT.Copy).then_inc(hi_done, 1)

        def split_lo(dve, c, i=0):
            if isinstance(i, int) and c + RING * i >= UNITS:
                return
            s = c % RING
            dve.wait_ge(hi_done, c + RING * i + 1)
            nc.vector.tensor_tensor(wlo[:, s], raw[:, s], whi[:, s].bitcast(F32),
                                    ALU.subtract).then_inc(lo_done, 1)

        def lo_rows(tensor_tensor, c, kk):
            s = c % RING
            return tensor_tensor(rows(wlo, s)[:, kk, :], rows(raw, s)[:, kk, :],
                                 rows(whi, s)[:, kk, :].bitcast(F32), ALU.subtract)

        def products(dst, ah, al, bh, bl, start, stop):
            nc.tensor.matmul(dst, ah, bh, start=start, stop=False)
            nc.tensor.matmul(dst, ah, bl, start=False, stop=False)
            return nc.tensor.matmul(dst, al, bh, start=False, stop=stop)

        def unit_ready(pe, c, i=0):
            pe.wait_ge(lo_done, c + RING * i + 1)

        def feature_tile(dst, c, j, ks=range(KD)):
            h, l = cols(whi, c % RING), cols(wlo, c % RING)
            for k in ks:
                last = products(dst, h[:, k, j * P:(j + 1) * P], l[:, k, j * P:(j + 1) * P],
                                xh[:, k, :], xl[:, k, :], k == 0, k == KD - 1)
            return last

        def out_rows(acc, ah, al, c, m, kk, first, last, columns=range(2)):
            h, l = rows(whi, c % RING), rows(wlo, c % RING)
            for n in columns:
                b = slice(n * BANK, (n + 1) * BANK)
                ins = products(ps[:, acc[m][n], :], ah[:, m * P:(m + 1) * P], al[:, m * P:(m + 1) * P],
                               h[:, kk, b], l[:, kk, b], first, last)
            return ins

        consts = {}

        block = ctx.enter_context(nc.Block())

        @block.sync
        def _(sp):
            def in_cols(w, at):
                return w[:, bass.ds(at, 256)].rearrange("(k p) n -> p k n", p=P)

            def in_rows(w, at):
                return w[bass.ds(at, 256), :].rearrange("(k p) n -> p k n", p=P)

            def ln_params(slot, n, g, b):
                for i, v in enumerate((g, b)):
                    sp.dma_start(lnp[:, slot, i, :], v.partition_broadcast(P)).then_inc(lnp_loaded[n], 16)

            for m in range(TT):
                for g in range(2):
                    b = slice(g * BANK, (g + 1) * BANK)
                    sp.dma_start(xtok[:, m, b], x[0, m * P:(m + 1) * P, b]).then_inc(x_loaded[2 * m + g], 16)
            for i, (u, k0, k1, _) in enumerate(PIECES):
                sp.dma_start(cols(raw, u)[:, k0:k1, :],
                             att_w_in[0, k0 * P:k1 * P, u * D:u * D + 256].rearrange("(k p) n -> p k n", p=P))\
                  .then_inc(piece_loaded[i], 16)
            load(sp, 2, 0, cols, in_cols(att_w_in[0], 2 * D))
            for l in range(2):
                sp.dma_start(stage[:, 4 * l:4 * l + 3, :],
                             ffn_conv_w[l].rearrange("w (f p) -> f w p", p=P)).then_inc(par_loaded, 16)
                sp.dma_start(stage[:, 4 * l + 3, :],
                             ffn_conv_b[l].rearrange("(f p) -> f p", p=P)).then_inc(par_loaded, 16)
            for i, v in enumerate((ret_gn_g, ret_gn_b)):
                sp.dma_start(gstage[:, i, :], v[0].rearrange("(f p) -> f p", p=P)).then_inc(par_loaded, 16)
            with sp.Fori(1, QUADS) as t:
                for j in range(3):
                    load(sp, j, t, cols, in_cols(att_w_in[0], t * 256 + j * D))
            ln_params(0, 0, mix_ln_g[0], mix_ln_b[0])
            for j in range(4):
                load(sp, U_ATT_OUT + j, 0, rows, in_rows(att_w_out[0], j * 256))
            ln_params(1, 1, ffn_ln_g[0], ffn_ln_b[0])

            def ffn_loads(l):
                u = U_FFN[l]
                load(sp, u, 0, cols, in_cols(ffn_w_up[l], 0))
                load(sp, u + 1, 0, cols, in_cols(ffn_w_up[l], FFN))
                with sp.Fori(1, PAIRS) as i:
                    load(sp, u - 1, i, cols, in_cols(ffn_w_up[l], i * 256))
                    load(sp, u, i, cols, in_cols(ffn_w_up[l], i * 256 + FFN))
                    load(sp, u + 1, i, rows, in_rows(ffn_w_down[l], i * 256 - 256))
                load(sp, u + 3 * PAIRS - 1, 0, rows, in_rows(ffn_w_down[l], FFN - 256))

            ffn_loads(0)
            sp.wait_ge(x_ready, 4)
            ln_params(0, 2, mix_ln_g[1], mix_ln_b[1])
            with sp.Fori(0, RH) as h:
                for j in range(2):
                    load(sp, U_RET + j, 2 * h, quarter,
                         ret_w_in[0][j * BANK:(j + 1) * BANK, bass.ds(h * RV + 2 * D, RV)]
                         .rearrange("(k p) n -> p k n", p=P))
                for j in range(2):
                    load(sp, U_RET + 2 + j, 2 * h, cols, in_cols(ret_w_in[0], h * RK + j * D))
                for j in range(2):
                    load(sp, U_RET + 4 + j, 2 * h, cols, in_cols(ret_w_in[0], h * RV + 4 * D + j * 256))
            for j in range(8):
                load(sp, U_RET_OUT + j, 0, rows, in_rows(ret_w_out[0], j * 256))
            sp.wait_ge(x_ready, 8)
            ln_params(1, 3, ffn_ln_g[1], ffn_ln_b[1])
            ffn_loads(1)
            for i, b in enumerate(OUT_PIECES):
                m = i // 2 if i < 4 else 1
                sp.wait_ge(x_ready, 12 + i + 1)
                sp.dma_start(out[0, m * P:(m + 1) * P, b], xtok[:, m, b]).then_inc(stored, 16)
            sp.wait_ge(stored, 16 * len(OUT_PIECES))

        @block.gpsimd
        def _(pool):
            n = [0]

            def step(ins):
                n[0] += 1
                ins.then_inc(const_step, 1)
                pool.wait_ge(const_step, n[0])

            step(nc.gpsimd.memset(ident[:], 0.0))
            step(nc.gpsimd.affine_select(out=ident[:], in_=ident[:], compare_op=ALU.not_equal, fill=1.0,
                                         base=0, pattern=[[-1, P]], channel_multiplier=1))
            for m, (a, b) in enumerate(((0, P), (P, CAUSAL))):
                step(nc.gpsimd.iota(dist[:, a:b], pattern=[[1, b - a]], base=-m * P, channel_multiplier=-1,
                                    allow_small_or_imprecise_dtypes=True))
                step(nc.gpsimd.affine_select(out=dist[:, a:b], in_=dist[:, a:b], compare_op=ALU.is_ge,
                                             fill=MASKED, base=m * P, pattern=[[-1, b - a]],
                                             channel_multiplier=1))
            for h in range(HEADS):
                nc.gpsimd.memset(slopes[:, h:h + 1], 2.0 ** (-8.0 * (h + 1) / HEADS))
            step(nc.gpsimd.memset(mhalf[:], -0.5))
            consts["attention"] = n[0]
            step(nc.gpsimd.iota(powers[:, 0:16], pattern=[[16, 16]], base=0, channel_multiplier=0,
                                allow_small_or_imprecise_dtypes=True))
            step(nc.gpsimd.iota(powers[:, 16:32], pattern=[[1, 16]], base=0, channel_multiplier=0,
                                allow_small_or_imprecise_dtypes=True))
            step(nc.gpsimd.iota(nkey[:], pattern=[[0, 1]], base=0, channel_multiplier=-1,
                                allow_small_or_imprecise_dtypes=True))
            for h in range(RH):
                step(nc.gpsimd.memset(gbase[:], 1.0 - 2.0 ** (-5.0 - h)))
                step(nc.gpsimd.tensor_tensor(gpow[:], gbase[:], powers[:], ALU.pow))
                step(nc.gpsimd.tensor_tensor(gkey[:, 0:1], gbase[:, 0:1], nkey[:], ALU.pow))
                step(nc.gpsimd.tensor_scalar(gkey[:, 1:2], gkey[:, 0:1], RK ** -0.5, None, ALU.mult))
                full = decay[:, h, 0:SEQ]
                step(nc.gpsimd.tensor_tensor(
                    full.rearrange("p (a b) -> p a b", a=16),
                    gpow[:, 0:16].unsqueeze(2).to_broadcast([P, 16, 16]),
                    gpow[:, 16:32].unsqueeze(1).to_broadcast([P, 16, 16]), ALU.mult))
                step(nc.gpsimd.tensor_scalar(full, full, gkey[:, 1:2], None, ALU.mult))
                step(nc.gpsimd.affine_select(out=full, in_=full, compare_op=ALU.is_ge, fill=0.0, base=0,
                                             pattern=[[1, SEQ]], channel_multiplier=-1))
                step(nc.gpsimd.tensor_copy(decay[:, h, SEQ:CAUSAL], decay[:, h, 0:P]))
            consts["retention"] = n[0]

            def inverse_root(n):
                for m in range(TT):
                    if (n, m) == (1, 1):
                        s = (U_RET + 1) % RING
                        pool.wait_ge(hi_done, U_RET + 2)
                        pool.wait_ge(lo_done, U_RET + 1)
                        nc.gpsimd.tensor_tensor(wlo[:, s], raw[:, s], whi[:, s].bitcast(F32),
                                                ALU.subtract).then_inc(lo_done, 1)
                    pool.wait_ge(veps_ready, TT * n + m + 1)
                    nc.gpsimd.tensor_tensor(rstd[:, m:m + 1], veps[:, m:m + 1], mhalf[:, 0:1],
                                            ALU.pow).then_inc(rstd_ready, 1)

            def ffn_pair(f, i):
                pool.wait_ge(f["gelu_done"], i + 1)
                pool.wait_ge(f["taps_done"], 2 * i + 2)
                if not isinstance(i, int) or i > 0:
                    pool.wait_ge(f["z_ready"], i)
                    pool.wait_ge(f["zh_done"], i)
                nc.gpsimd.tensor_tensor(zf[:], ga[:], ug[:], ALU.mult).then_inc(f["mult_done"], 1)
                pool.wait_ge(f["zh_done"], i + 1)
                nc.gpsimd.tensor_tensor(zl[:, 0], zf[:], zh[:, 0].bitcast(F32),
                                        ALU.subtract).then_inc(f["z_ready"], 1)

            def ffn_all(l):
                ffn_pair(ffn[l], 0)
                with pool.Fori(1, PAIRS - 1) as i:
                    ffn_pair(ffn[l], i)
                c = U_FFN[l] + 3 * PAIRS - 1
                pool.wait_ge(hi_done, c + 1)
                pool.wait_ge(lo_half, l + 1)
                lo_rows(nc.gpsimd.tensor_tensor, c, 1).then_inc(lo_done, 1)

            inverse_root(0)
            ffn_all(0)
            inverse_root(1)
            with pool.Fori(0, RH) as h:
                pool.wait_ge(gvar_ready, h + 1)
                nc.gpsimd.tensor_tensor(rstd[:], veps[:], mhalf[:], ALU.pow).then_inc(grstd_ready, 1)
                pool.wait_ge(ro_hi, h + 1)
                nc.gpsimd.tensor_tensor(ol[:, bass.ds(4 * h, 4), :], ygn[:],
                                        oh[:, bass.ds(4 * h, 4), :].bitcast(F32),
                                        ALU.subtract).then_inc(ro_lo, 1)
            inverse_root(2)
            ffn_all(1)
            inverse_root(3)

        @block.scalar
        def _(act):
            def turned_hi(n, tr, *parts):
                for m, g in parts or TILE_HALVES:
                    act.wait_ge(xt_turned, 4 * n + 2 * m + g + 1)
                    nc.scalar.activation(
                        xh[:, 4 * g:4 * g + 4, m * P:(m + 1) * P],
                        ps[:, tr[m][g], :].rearrange("p (k n) -> p k n", k=4), ACT.Copy
                    ).then_inc(xh_ready, 1)

            def variance(n, m):
                act.wait_ge(mean_ready, TT * n + m + 1)
                if n or m:
                    act.wait_ge(var_ready, TT * n + m)
                nc.scalar.activation(squares, xtok[:, m, :], ACT.Square, bias=nmean[:, m:m + 1],
                                     accum_out=var[:, m:m + 1]).then_inc(var_ready, 1)

            def copy_tiles(dst, u, t, scale):
                if isinstance(t, int) and t == 0:
                    for j in range(2):
                        ins = nc.scalar.activation(dst[:, j, :], apart(u, j), ACT.Copy, scale=scale)
                    return ins
                return nc.scalar.activation(dst[:], halves(u), ACT.Copy, scale=scale)

            def q_copy(t):
                act.wait_ge(used, RING * t + 1)
                if not isinstance(t, int) or t > 0:
                    act.wait_ge(s_ready, 4 * t)
                copy_tiles(qT, 0, t, HD ** -0.5).then_inc(q_copied, 1)

            def k_copy(t):
                act.wait_ge(used, RING * t + 2)
                copy_tiles(kT, 1, t, 1.0).then_inc(k_copied, 1)

            def exps(t, h):
                act.wait_ge(max_ready, 4 * t + h + 1)
                for m, (a, b) in enumerate(((0, P), (P, CAUSAL))):
                    last = nc.scalar.activation(sc[:, h % 2, a:b], sc[:, h % 2, a:b], ACT.Exp,
                                                bias=nmax[:, h, m:m + 1], accum_out=rsum[:, h, m:m + 1])
                last.then_inc(exp_ready, 1)

            def pt_copy(t, h):
                act.wait_ge(p_turned, 4 * t + h + 1)
                if h >= 2:
                    act.wait_ge(pv_done, 4 * t + h - 1)
                nc.scalar.activation(pt[:, h % 2, :], ps[:, 5 + h % 2, 0:CAUSAL], ACT.Copy)\
                    .then_inc(pt_ready, 1)

            def out_hi(t, pair):
                act.wait_ge(pv_done, 4 * t + 2 * pair + 2)
                nc.scalar.activation(oh[:, bass.ds(2 * t + pair, 1), :], halves(7)[:, pair:pair + 1, :],
                                     ACT.Copy).then_inc(o_hi, 1)

            def quad(t, core, copies):
                split_hi(act, U_ATT + 2, t)
                exps(core, 0)
                exps(core, 1)
                pt_copy(core, 0)
                pt_copy(core, 1)
                split_hi(act, U_ATT + 3, t)
                exps(core, 2)
                exps(core, 3)
                out_hi(core, 0)
                if copies:
                    q_copy(t)
                if copies:
                    split_hi(act, U_ATT + 4, t)
                    k_copy(t)
                pt_copy(core, 2)
                pt_copy(core, 3)
                out_hi(core, 1)
                if not copies:
                    split_hi(act, U_ATT + 4, t)

            def piece_hi_part(i):
                u, k0, k1, whole = PIECES[i]
                act.wait_ge(piece_loaded[i], 16)
                nc.scalar.activation(cols(whi, u)[:, k0:k1, :], cols(raw, u)[:, k0:k1, :], ACT.Copy)\
                  .then_inc(hi_done if whole else piece_hi, 1)

            turned_hi(0, TR_IN, (0, 0), (0, 1), (1, 0))
            piece_hi_part(0)
            turned_hi(0, TR_IN, (1, 1))
            for i in range(1, len(PIECES)):
                piece_hi_part(i)
            split_hi(act, 2)
            split_hi(act, 3)
            q_copy(0)
            split_hi(act, 4)
            k_copy(0)
            act.wait_ge(par_turned, 1)
            nc.scalar.activation(par[:], ps[:, 7, 0:par.shape[1]], ACT.Copy).then_inc(par_copied, 1)
            with act.Fori(1, QUADS) as t:
                quad(t, t - 1, True)
            quad(QUADS, QUADS - 1, False)
            variance(0, 0)
            split_hi(act, U_ATT_OUT + 5)
            variance(0, 1)
            turned_hi(1, TR_ATT)

            def conv_tap(l, i, part, u, s):
                if part == 1 and isinstance(i, int) and (i, s) == (PAIRS - 1, 0):
                    act.wait_ge(ffn[l]["last_gate"], 1)
                else:
                    act.wait_ge(used, up_unit(l, i, part) + RING * i + 1)
                at = part * (FT // 2) + 2 * i + s
                nc.scalar.activation(u[:, s, :], up_bank(part, s), ACT.Identity,
                                     bias=par[:, bass.ds(tap(l, 3) + at, 1)],
                                     scale=par[:, bass.ds(tap(l, 2) + at, 1)]).then_inc(ffn[l]["scaled"], 1)

            def ffn_conv(l, i, part, u):
                f = ffn[l]
                if not isinstance(i, int) or i > 0:
                    act.wait_ge(f["gelu_done"] if part == 0 else f["mult_done"], i)
                if isinstance(i, int) and i == 0 and l == 0 and part == 0:
                    act.wait_ge(par_copied, 1)
                for s in range(2):
                    conv_tap(l, i, part, u, s)

            def gelu(l, i):
                f = ffn[l]
                act.wait_ge(f["taps_done"], 2 * i + 1)
                if not isinstance(i, int) or i > 0:
                    act.wait_ge(f["mult_done"], i)
                nc.scalar.activation(ga[:], ua[:], ACT.Gelu).then_inc(f["gelu_done"], 1)

            def z_hi(l, i):
                f = ffn[l]
                act.wait_ge(f["mult_done"], i + 1)
                act.wait_ge(used, U_FFN[l] + 2 + RING * i)
                nc.scalar.activation(zh[:, 0], zf[:], ACT.Copy).then_inc(f["zh_done"], 1)

            def ffn_iter(l, i):
                u = U_FFN[l]
                z_hi(l, i - 1)
                split_hi(act, u + 1, i)
                ffn_conv(l, i, 0, ua)
                split_hi(act, u + 2, i)
                gelu(l, i)

            def ffn_all(l):
                split_hi(act, U_FFN[l] + 2)
                ffn_conv(l, 0, 0, ua)
                split_hi(act, U_FFN[l] + 3)
                gelu(l, 0)
                ffn_conv(l, 0, 1, ug)
                with act.Fori(1, PAIRS - 1) as i:
                    ffn_iter(l, i)
                    ffn_conv(l, i, 1, ug)
                    split_hi(act, U_FFN[l] + 3, i)
                ffn_iter(l, PAIRS - 1)
                f = ffn[l]
                act.wait_ge(f["mult_done"], PAIRS - 1)
                for s in range(2):
                    conv_tap(l, PAIRS - 1, 1, ug, s)
                    if s == 1:
                        split_hi(act, U_FFN[l] + 3 * PAIRS)
                    act.wait_ge(f["mult_done"], PAIRS + s)
                    nc.scalar.activation(zh[:, 1, s], zf[:, s], ACT.Copy).then_inc(f["zh_done"], 1)

            ffn_all(0)
            variance(1, 0)
            split_hi(act, U_RET + 1)
            turned_hi(2, TR_FFN, (0, 0), (0, 1))
            split_hi(act, U_RET + 2)
            variance(1, 1)
            turned_hi(2, TR_FFN, (1, 0), (1, 1))

            def ret_gain(h, banks):
                act.wait_ge(on_turned, h + 1)
                act.wait_ge(ro_lo, h + 1)
                for j in range(4):
                    nc.scalar.activation(ygn[:, j, :], halves(banks[j // 2])[:, j % 2, :], ACT.Identity,
                                         bias=par[:, bass.ds(4 * h + (GN + 2 * KD + j), 1)],
                                         scale=par[:, bass.ds(4 * h + (GN + j), 1)]).then_inc(y_ready, 1)

            def ret_hi(h):
                act.wait_ge(gated, h + 1)
                nc.scalar.activation(oh[:, bass.ds(4 * h, 4), :], ygn[:], ACT.Copy).then_inc(ro_hi, 1)

            def ret_head(h, before):
                if before:
                    split_hi(act, U_RET + 2, 2 * h)
                split_hi(act, U_RET + 3, 2 * h)
                if before:
                    ret_gain(h - 1, (4, 5))
                act.wait_ge(used, U_RET + 6 * h + 2)
                for m in range(TT):
                    nc.scalar.activation(vh[:, m, :], ps[:, 2 + m, :], ACT.Copy).then_inc(rv_hi, 1)
                if before:
                    ret_hi(h - 1)
                split_hi(act, U_RET + 4, 2 * h)
                act.wait_ge(used, U_RET + 6 * h + 3)
                nc.scalar.activation(qT[:], halves(0), ACT.Copy).then_inc(rq_copied, 1)
                split_hi(act, U_RET + 5, 2 * h)
                act.wait_ge(used, U_RET + 6 * h + 4)
                nc.scalar.activation(kT[:], halves(1), ACT.Copy).then_inc(rk_copied, 1)
                split_hi(act, U_RET + 6, 2 * h)
                act.wait_ge(decayed, h + 1)
                nc.scalar.activation(sh[:], pt[:, 0, :], ACT.Copy).then_inc(decayed_hi, 1)
                act.wait_ge(used, U_RET + 6 * h + 5)
                nc.scalar.activation(sg[:, 0:2, :], halves(4), ACT.Silu).then_inc(silu_done, 1)
                split_hi(act, U_RET + 7, 2 * h)
                act.wait_ge(used, U_RET + 6 * h + 6)
                nc.scalar.activation(sg[:, 2:4, :], halves(5), ACT.Silu).then_inc(silu_done, 1)

            ret_head(0, False)
            with act.Fori(1, RH) as h:
                ret_head(h, True)
            split_hi(act, U_RET_OUT + 2)
            split_hi(act, U_RET_OUT + 3)
            ret_gain(RH - 1, (2, 3))
            split_hi(act, U_RET_OUT + 4)
            ret_hi(RH - 1)
            for j in range(5, 9):
                split_hi(act, U_RET_OUT + j)
            variance(2, 0)
            split_hi(act, U_RET_OUT + 9)
            variance(2, 1)
            turned_hi(3, TR_RET)
            ffn_all(1)
            variance(3, 0)
            variance(3, 1)

        @block.vector
        def _(dve):
            def turned_lo(n, tr, *parts):
                for m, g in parts or TILE_HALVES:
                    dve.wait_ge(xh_ready, 4 * n + 2 * m + g + 1)
                    ks, ts = slice(4 * g, 4 * g + 4), slice(m * P, (m + 1) * P)
                    nc.vector.tensor_tensor(
                        xl[:, ks, ts], ps[:, tr[m][g], :].rearrange("p (k n) -> p k n", k=4),
                        xh[:, ks, ts].bitcast(F32), ALU.subtract).then_inc(xl_ready, 1)

            steps = [0]

            def step(ins):
                steps[0] += 1
                ins.then_inc(dve_ln, 1)

            def settle():
                dve.wait_ge(dve_ln, steps[0])

            def residual(n, m, c, acc):
                if (m, c) == (1, 1):
                    dve.wait_ge(used, LAST_UNIT[n] + 1)
                else:
                    dve.wait_ge(acc_ready, 2 * n + m + 1)
                half = xtok[:, m, c * BANK:(c + 1) * BANK]
                step(nc.vector.scalar_tensor_tensor(out=half, in0=half, scalar=ALPHA,
                                                    in1=ps[:, acc[m][c], :], op0=ALU.mult, op1=ALU.add,
                                                    accum_out=half_sum[:, m, c:c + 1]))

            def mean(n, m):
                settle()
                nc.vector.tensor_scalar(nmean[:, m:m + 1], half_sum[:, m, 0:1], half_sum[:, m, 1:2],
                                        -1.0 / D, ALU.add, ALU.mult).then_inc(mean_ready, 1)

            def centre(n, m):
                if m == 0:
                    dve.wait_ge(lnp_loaded[n], 32)
                dve.wait_ge(mean_ready, TT * n + m + 1)
                step(nc.vector.scalar_tensor_tensor(out=lnt[:, m, :], in0=xtok[:, m, :],
                                                    scalar=nmean[:, m:m + 1], in1=lnp[:, n % 2, 0, :],
                                                    op0=ALU.add, op1=ALU.mult))
                dve.wait_ge(var_ready, TT * n + m + 1)
                nc.vector.tensor_scalar(veps[:, m:m + 1], var[:, m:m + 1], 1.0 / D, LN_EPS, ALU.mult, ALU.add)\
                    .then_inc(veps_ready, 1)

            def normal(n, m, c):
                settle()
                dve.wait_ge(rstd_ready, TT * n + m + 1)
                write_normal(n, m, slice(c * BANK, (c + 1) * BANK))

            def write_normal(n, m, b):
                nc.vector.scalar_tensor_tensor(out=xtok[:, m, b], in0=lnt[:, m, b],
                                               scalar=rstd[:, m:m + 1], in1=lnp[:, n % 2, 1, b],
                                               op0=ALU.mult, op1=ALU.add).then_inc(x_ready, 1)

            def layer_norm(n, acc):
                residual(n, 0, 0, acc)
                residual(n, 0, 1, acc)
                mean(n, 0)
                centre(n, 0)
                residual(n, 1, 0, acc)
                normal(n, 0, 0)
                residual(n, 1, 1, acc)
                mean(n, 1)
                centre(n, 1)
                normal(n, 0, 1)
                normal(n, 1, 0)
                if n < 3:
                    normal(n, 1, 1)
                else:
                    for b in OUT_PIECES[3:]:
                        write_normal(n, 1, b)

            def scores(t, h):
                g = 4 * t + h
                dve.wait_ge(s_ready, g + 1)
                if h >= 2:
                    dve.wait_ge(p_turned, g - 1)
                nc.vector.scalar_tensor_tensor(out=sc[:, h % 2, :], in0=dist[:], scalar=slopes[:, bass.ds(g, 1)],
                                               in1=ps[:, score_bank(t, h), 0:CAUSAL], op0=ALU.mult,
                                               op1=ALU.add).then_inc(biased, 1)
                dve.wait_ge(biased, g + 1)
                for m, (a, b) in enumerate(((0, P), (P, CAUSAL))):
                    last = nc.vector.tensor_reduce(nmax[:, h, m:m + 1], sc[:, h % 2, a:b], AX_X, ALU.max,
                                                   negate=True)
                last.then_inc(max_ready, 1)

            def normalise(t, h):
                g = 4 * t + h
                dve.wait_ge(exp_ready, g + 1)
                nc.vector.reciprocal(rinv[:, h, :], rsum[:, h, :]).then_inc(inv_ready, 1)
                dve.wait_ge(inv_ready, g + 1)
                for m, (a, b) in enumerate(((0, P), (P, CAUSAL))):
                    last = nc.vector.tensor_scalar(sc[:, h % 2, a:b], sc[:, h % 2, a:b], rinv[:, h, m:m + 1],
                                                   None, ALU.mult)
                last.then_inc(p_ready, 1)

            def out_lo(t, pair):
                dve.wait_ge(o_hi, 2 * t + pair + 1)
                at = bass.ds(2 * t + pair, 1)
                nc.vector.tensor_tensor(ol[:, at, :], halves(7)[:, pair:pair + 1, :],
                                        oh[:, at, :].bitcast(F32), ALU.subtract).then_inc(o_lo, 1)

            def v_copy(t):
                dve.wait_ge(used, RING * t + 3)
                if not isinstance(t, int) or t > 0:
                    dve.wait_ge(pv_done, 4 * t)
                nc.vector.tensor_copy(vt[:], halves(2)).then_inc(v_copied, 1)

            def quad(t, core, copies):
                scores(core, 0)
                scores(core, 1)
                normalise(core, 0)
                normalise(core, 1)
                split_lo(dve, U_ATT + 2, t)
                scores(core, 2)
                scores(core, 3)
                split_lo(dve, U_ATT + 3, t)
                normalise(core, 2)
                normalise(core, 3)
                out_lo(core, 0)
                if copies:
                    split_lo(dve, U_ATT + 4, t)
                out_lo(core, 1)
                if not copies:
                    split_lo(dve, U_ATT + 4, t)
                if copies:
                    v_copy(t)

            nc.vector.memset(st6[:], 0.0).then_inc(o_lo, 1)
            nc.vector.memset(var[:], 0.0).then_inc(ro_lo, 1)

            def piece_lo_part(i):
                u, k0, k1, whole = PIECES[i]
                if whole:
                    dve.wait_ge(hi_done, u + 1)
                else:
                    dve.wait_ge(piece_hi, 1 + sum(not p[3] for p in PIECES[:i]))
                nc.vector.tensor_tensor(cols(wlo, u)[:, k0:k1, :], cols(raw, u)[:, k0:k1, :],
                                        cols(whi, u)[:, k0:k1, :].bitcast(F32), ALU.subtract)\
                  .then_inc(lo_done if whole else piece_lo, 1)

            turned_lo(0, TR_IN, (0, 0), (0, 1), (1, 0))
            piece_lo_part(0)
            turned_lo(0, TR_IN, (1, 1))
            for i in range(1, len(PIECES)):
                piece_lo_part(i)
            split_lo(dve, 2)
            split_lo(dve, 3)
            split_lo(dve, 4)
            v_copy(0)
            dve.wait_ge(const_step, consts["attention"])
            with dve.Fori(1, QUADS) as t:
                quad(t, t - 1, True)
            quad(QUADS, QUADS - 1, False)
            layer_norm(0, ACC_ATT)
            turned_lo(1, TR_ATT)
            split_lo(dve, U_ATT_OUT + 5)

            def conv_tap(l, i, part, u, s, back):
                f = ffn[l]
                if back == 1:
                    dve.wait_ge(f["scaled"], 4 * i + 2 * part + s + 1)
                else:
                    dve.wait_ge(f["tap1"], 4 * i + 2 * part + s + 1)
                at = part * (FT // 2) + 2 * i + s
                ins = nc.vector.scalar_tensor_tensor(
                    out=u[:, s, back:SEQ], in0=up_bank(part, s)[:, 0:SEQ - back],
                    scalar=par[:, bass.ds(tap(l, 2 - back) + at, 1)], in1=u[:, s, back:SEQ],
                    op0=ALU.mult, op1=ALU.add)
                if back == 1:
                    ins.then_inc(f["tap1"], 1)
                return ins

            def ffn_taps(l, i, part, u):
                for back in (1, 2):
                    for s in range(2):
                        last = conv_tap(l, i, part, u, s, back)
                last.then_inc(ffn[l]["taps_done"], 1)

            def ffn_iter(l, i):
                u = U_FFN[l]
                split_lo(dve, u + 1, i)
                ffn_taps(l, i, 0, ua)

            def ffn_all(l):
                split_lo(dve, U_FFN[l] + 2)
                ffn_taps(l, 0, 0, ua)
                split_lo(dve, U_FFN[l] + 3)
                ffn_taps(l, 0, 1, ug)
                with dve.Fori(1, PAIRS - 1) as i:
                    ffn_iter(l, i)
                    split_lo(dve, U_FFN[l] + 2, i)
                    ffn_taps(l, i, 1, ug)
                    split_lo(dve, U_FFN[l] + 3, i)
                ffn_iter(l, PAIRS - 1)
                dve.wait_ge(hi_done, U_FFN[l] + 3 * PAIRS)
                lo_rows(nc.vector.tensor_tensor, U_FFN[l] + 3 * PAIRS - 1, 0).then_inc(lo_half, 1)
                f = ffn[l]
                for s in range(2):
                    conv_tap(l, PAIRS - 1, 1, ug, s, 1)
                    conv_tap(l, PAIRS - 1, 1, ug, s, 2).then_inc(f["last_taps"], 1)
                    if s == 0:
                        dve.wait_ge(f["gelu_done"], PAIRS)
                        dve.wait_ge(f["zh_done"], PAIRS - 1)
                        dve.wait_ge(f["z_ready"], PAIRS - 1)
                    dve.wait_ge(f["last_taps"], s + 1)
                    nc.vector.tensor_tensor(zf[:, s], ga[:, s], ug[:, s], ALU.mult).then_inc(f["mult_done"], 1)
                    dve.wait_ge(f["zh_done"], PAIRS + s)
                    nc.vector.tensor_tensor(zl[:, 1, s], zf[:, s], zh[:, 1, s].bitcast(F32),
                                            ALU.subtract).then_inc(f["z_ready"], 1)
                dve.wait_ge(lo_done, U_FFN[l] + 3 * PAIRS)
                split_lo(dve, U_FFN[l] + 3 * PAIRS)

            ffn_all(0)
            residual(1, 0, 0, ACC_FFN)
            residual(1, 0, 1, ACC_FFN)
            mean(1, 0)
            centre(1, 0)
            normal(1, 0, 0)
            normal(1, 0, 1)
            residual(1, 1, 0, ACC_FFN)
            turned_lo(2, TR_FFN, (0, 0), (0, 1))
            residual(1, 1, 1, ACC_FFN)
            mean(1, 1)
            centre(1, 1)
            normal(1, 1, 0)
            normal(1, 1, 1)
            turned_lo(2, TR_FFN, (1, 0), (1, 1))
            dve.wait_ge(lo_done, U_RET + 2)

            GN_STEPS = TT + 2
            dve.wait_ge(const_step, consts["retention"])
            def ret_gate(h):
                dve.wait_ge(y_ready, 4 * h + 4)
                dve.wait_ge(silu_done, 2 * h + 2)
                nc.vector.tensor_tensor(ygn[:], ygn[:], sg[:], ALU.mult).then_inc(gated, 1)

            def ret_head(h, before):
                split_lo(dve, U_RET + 2, 2 * h)
                split_lo(dve, U_RET + 3, 2 * h)
                if before:
                    ret_gate(h - 1)
                for m in range(TT):
                    dve.wait_ge(rv_hi, TT * h + m + 1)
                    nc.vector.tensor_tensor(vl[:, m, :], ps[:, 2 + m, :], vh[:, m, :].bitcast(F32),
                                            ALU.subtract).then_inc(rv_lo, 1)
                for j in range(4, 7):
                    split_lo(dve, U_RET + j, 2 * h)
                dve.wait_ge(rs_ready, h + 1)
                nc.vector.tensor_tensor(pt[:, 0:1, :], ps[:, 6:7, 0:CAUSAL], decay[:, bass.ds(h, 1), :],
                                        ALU.mult).then_inc(decayed, 1)
                dve.wait_ge(decayed_hi, h + 1)
                nc.vector.tensor_tensor(sl[:], pt[:, 0, :], sh[:].bitcast(F32), ALU.subtract).then_inc(decayed_lo, 1)
                split_lo(dve, U_RET + 7, 2 * h)
                for m, bank in enumerate((7, 0)):
                    dve.wait_ge(ro_ready, TT * h + m + 1)
                    nc.vector.bn_stats(st6[:, m, :], ps[:, bank, :]).then_inc(dve_gn, 1)
                st = [st6[:, :, i] for i in range(6)]
                dve.wait_ge(dve_gn, GN_STEPS * h + TT)
                nc.vector.tensor_tensor(gm[:, 0, :], st[1], st[4], ALU.add)
                nc.vector.tensor_tensor(gm[:, 1, :], st[1], st[4], ALU.subtract)
                nc.vector.tensor_tensor(gm[:, 2, :], st[2], st[5], ALU.add).then_inc(dve_gn, 1)
                dve.wait_ge(dve_gn, GN_STEPS * h + TT + 1)
                nc.vector.tensor_scalar(gmean[:], gm[:, 0, :], 0.5, None, ALU.mult)
                nc.vector.scalar_tensor_tensor(out=gm[:, 3, :], in0=gm[:, 1, :], scalar=0.25, in1=gm[:, 1, :],
                                               op0=ALU.mult, op1=ALU.mult)
                nc.vector.tensor_scalar(gm[:, 4, :], gm[:, 2, :], 1.0 / RV, GN_EPS, ALU.mult, ALU.add)\
                    .then_inc(dve_gn, 1)
                dve.wait_ge(dve_gn, GN_STEPS * h + TT + 2)
                nc.vector.tensor_tensor(veps[:], gm[:, 3, :], gm[:, 4, :], ALU.add).then_inc(gvar_ready, 1)
                dve.wait_ge(grstd_ready, h + 1)
                for m, bank in enumerate((7, 0)):
                    nc.vector.tensor_scalar(onrm[:, m, :], ps[:, bank, :], gmean[:, m:m + 1], rstd[:, m:m + 1],
                                            ALU.subtract, ALU.mult).then_inc(on_ready, 1)

            ret_head(0, False)
            with dve.Fori(1, RH) as h:
                ret_head(h, True)
            split_lo(dve, U_RET_OUT + 2)
            split_lo(dve, U_RET_OUT + 3)
            ret_gate(RH - 1)
            for j in range(4, 9):
                split_lo(dve, U_RET_OUT + j)
            layer_norm(2, ACC_RET)
            turned_lo(3, TR_RET)
            split_lo(dve, U_RET_OUT + 9)
            ffn_all(1)
            layer_norm(3, ACC_FFN)

        @block.tensor
        def _(pe):
            def keep_clock(bank, count):
                for _ in range(count):
                    nc.tensor.matmul(ps[:, bank, 0:P], ident[:], ident[:], start=True, stop=True)

            def turn_x(m, tr, n=None):
                for g in range(2):
                    if n is None:
                        pe.wait_ge(x_loaded[2 * m + g], 16)
                    else:
                        pe.wait_ge(x_ready, 4 * n + 2 * m + g + 1)
                    for k in range(4):
                        last = nc.tensor.transpose(ps[:, tr[m][g], k * P:(k + 1) * P],
                                                   xtok[:, m, (4 * g + k) * P:(4 * g + k + 1) * P], ident[:])
                    last.then_inc(xt_turned, 1)

            def last_unit(product):
                for n in range(2):
                    for kk in range(2):
                        last = product(kk, n)
                    last.then_inc(used if n else acc_ready, 1)

            def turn_after_ln(n, tr):
                keep_clock(tr[0][0], 14)
                for m in range(TT):
                    turn_x(m, tr, n)

            def x_parts(n, m, g):
                pe.wait_ge(xl_ready, 4 * (n + 1) + 2 * m + g + 1)

            def project_chunk(t, x_):
                u, j, half = x_ // 4, x_ // 2 % 2, x_ % 2
                if x_ % 4 == 0:
                    unit_ready(pe, U_ATT + u, t)
                    if not isinstance(t, int) or t > 0:
                        pe.wait_ge((q_copied, k_copied, v_copied)[u], t)
                ks = range(4 * half, 4 * half + 4)
                if u < 2:
                    last = feature_tile(halves(u)[:, j, :], u, j, ks)
                else:
                    h, l = cols(whi, u), cols(wlo, u)
                    for k in ks:
                        last = products(halves(2)[:, j, :], xh[:, k, j * P:(j + 1) * P],
                                        xl[:, k, j * P:(j + 1) * P], h[:, k, :], l[:, k, :],
                                        k == 0, k == KD - 1)
                if x_ % 4 == 3:
                    last.then_inc(used, 1)

            def head_rows(h):
                return slice(HD * (h % 2), HD * (h % 2) + HD), h // 2

            def score(t, h):
                rs, pair = head_rows(h)
                if h == 0:
                    pe.wait_ge(q_copied, t + 1)
                    pe.wait_ge(k_copied, t + 1)
                if h >= 2:
                    pe.wait_ge(biased, 4 * t + h - 1)
                if isinstance(t, int) and t == QUADS - 1 and h == 3:
                    pe.wait_ge(pt_ready, 4 * t + 1)
                bank = ps[:, score_bank(t, h), :]
                nc.tensor.matmul(bank[:, 0:P], qT[rs, pair, 0:P], kT[rs, pair, 0:P], start=True, stop=True)
                nc.tensor.matmul(bank[:, P:CAUSAL], qT[rs, pair, P:SEQ], kT[rs, pair, :],
                                 start=True, stop=True).then_inc(s_ready, 1)

            def turn_p(t, h):
                pe.wait_ge(p_ready, 4 * t + h + 1)
                for b in range(3):
                    last = nc.tensor.transpose(ps[:, 5 + h % 2, b * P:(b + 1) * P],
                                               sc[:, h % 2, b * P:(b + 1) * P], ident[:])
                last.then_inc(p_turned, 1)

            def values(t, pair):
                hs = (2 * pair, 2 * pair + 1)
                if pair == 0:
                    pe.wait_ge(v_copied, t + 1)
                    pe.wait_ge(par_copied, 1)
                pe.wait_ge(o_lo, 2 * t + pair + 1)
                for h in hs:
                    pe.wait_ge(pt_ready, 4 * t + h + 1)
                    nc.tensor.matmul(halves(7)[head_rows(h)[0], pair, :], vt[:, 0, h * HD:(h + 1) * HD],
                                     pt[:, h % 2, 0:SEQ], start=True, stop=False)
                for h in hs:
                    nc.tensor.matmul(halves(7)[head_rows(h)[0], pair, P:SEQ], vt[:, 1, h * HD:(h + 1) * HD],
                                     pt[:, h % 2, SEQ:CAUSAL], start=False, stop=True).then_inc(pv_done, 1)

            def core(t, x_, last=False):
                at_score, at_turn, at_values = ((0, 4), (3, 7), (5, 9)) if last else ((0, 5), (4, 9), (6, 11))
                for pair in range(2):
                    if x_ == at_score[pair]:
                        score(t, 2 * pair)
                        score(t, 2 * pair + 1)
                    if x_ == at_turn[pair]:
                        turn_p(t, 2 * pair)
                        turn_p(t, 2 * pair + 1)
                    if x_ == at_values[pair]:
                        values(t, pair)

            pe.wait_ge(const_step, 2)
            keep_clock(7, 4)
            for m in range(TT):
                turn_x(m, TR_IN)
            for i, (u, k0, k1, whole) in enumerate(PIECES):
                if whole:
                    unit_ready(pe, u)
                else:
                    pe.wait_ge(piece_lo, 1 + sum(not p[3] for p in PIECES[:i]))
                if i < 2:
                    x_parts(-1, 1, 0)
                else:
                    x_parts(-1, 1, 1)
                for j in range(2):
                    last = feature_tile(apart(u, j), u, j, range(k0, k1))
                if whole:
                    last.then_inc(used, 1)
            for x_ in range(8, 12):
                project_chunk(0, x_)
            pe.wait_ge(par_loaded, 16 * 6)
            for i in range(8):
                nc.tensor.transpose(ps[:, 7, i * FT:(i + 1) * FT], stage[:, i, :], ident[0:FT, 0:FT])
            for i in range(2):
                last = nc.tensor.transpose(ps[:, 7, GN + i * 2 * KD:GN + (i + 1) * 2 * KD], gstage[:, i, :],
                                           ident[0:2 * KD, 0:2 * KD])
            last.then_inc(par_turned, 1)
            with pe.Fori(1, QUADS) as t:
                for x_ in range(12):
                    core(t - 1, x_)
                    project_chunk(t, x_)
            def att_out(j, m, kk, columns=range(2)):
                k = 2 * j + kk
                return out_rows(ACC_ATT, oh[:, k, :], ol[:, k, :], U_ATT_OUT + j, m, kk, k == 0,
                                k == KD - 1, columns)

            order = [(j, m, kk) for j in range(2) for m in range(TT) for kk in range(2)]
            order += [(j, m, kk) for m in range(TT) for j in (2, 3) for kk in range(2)]
            for x_, (j, m, kk) in enumerate(order[:-2]):
                core(QUADS - 1, x_, last=True)
                if x_ == 2:
                    pe.wait_ge(v_copied, QUADS)
                if (m, kk) == (0, 0):
                    unit_ready(pe, U_ATT_OUT + j)
                    pe.wait_ge(o_lo, 1 + 2 * (QUADS - 1) if j < 3 else 1 + 2 * QUADS)
                last = att_out(j, m, kk)
                if (j, m, kk) == (3, 0, 1):
                    last.then_inc(acc_ready, 1)
                if (m, kk) == (1, 1):
                    last.then_inc(used, 1)
            last_unit(lambda kk, n: att_out(3, 1, kk, [n]))
            turn_after_ln(0, TR_ATT)

            def first_tile(dst, c, j, after_ln):
                h, l = cols(whi, c % RING), cols(wlo, c % RING)
                for n, (w, x_, ready) in enumerate(((h, xh, xh_ready), (l, xh, xh_ready), (h, xl, xl_ready))):
                    for k in range(KD):
                        if n != 1 and k % 4 == 0:
                            pe.wait_ge(ready, 4 * (after_ln + 1) + 2 + k // 4 + 1)
                        nc.tensor.matmul(dst, w[:, k, j * P:(j + 1) * P], x_[:, k, :],
                                         start=n == 0 and k == 0, stop=n == 2 and k == KD - 1)

            def up_pair(l, i, part, after_ln=None):
                c = up_unit(l, i, part)
                unit_ready(pe, c, i)
                if not isinstance(i, int) or i > 0:
                    pe.wait_ge(ffn[l]["taps_done"], 2 * i + part - 1)
                if after_ln is None:
                    last = feature_tile(up_bank(part, 0), c, 0)
                else:
                    first_tile(up_bank(part, 0), c, 0, after_ln)
                if part == 1 and isinstance(i, int) and i == PAIRS - 1:
                    last.then_inc(ffn[l]["last_gate"], 1)
                feature_tile(up_bank(part, 1), c, 1).then_inc(used, 1)

            def down(l, c, m, kk, z=0, first=False, last=False, columns=range(2)):
                return out_rows(ACC_FFN, zh[:, z, kk, :], zl[:, z, kk, :], c, m, kk,
                                first and kk == 0, last and kk == 1, columns)

            def down_pair(l, i, first=False):
                c = U_FFN[l] + 1
                unit_ready(pe, c, i)
                pe.wait_ge(ffn[l]["z_ready"], i)
                for m in range(TT):
                    for kk in range(2):
                        ins = down(l, c, m, kk, first=first)
                ins.then_inc(used, 1)

            def ffn_all(l, after_ln):
                up_pair(l, 0, 0, after_ln)
                up_pair(l, 0, 1)
                up_pair(l, 1, 0)
                up_pair(l, 1, 1)
                down_pair(l, 1, first=True)
                with pe.Fori(2, PAIRS - 1) as i:
                    up_pair(l, i, 0)
                    up_pair(l, i, 1)
                    down_pair(l, i)
                up_pair(l, PAIRS - 1, 0)
                up_pair(l, PAIRS - 1, 1)
                cs = [U_FFN[l] + 3 * PAIRS - 2, U_FFN[l] + 3 * PAIRS - 1]
                for z, c in enumerate(cs):
                    for kk in range(2):
                        if (z, kk) == (1, 0):
                            pe.wait_ge(lo_half, l + 1)
                        else:
                            unit_ready(pe, c)
                        pe.wait_ge(ffn[l]["z_ready"], PAIRS + kk if z else PAIRS - 1)
                        last = down(l, c, 0, kk, z, last=z == 1)
                last.then_inc(acc_ready, 1)
                for kk in range(2):
                    last = down(l, cs[0], 1, kk)
                last.then_inc(used, 1)
                last_unit(lambda kk, n: down(l, cs[1], 1, kk, 1, last=True, columns=[n]))

            ffn_all(0, 0)

            def ret_v(h, j, tiles=range(TT), ks=range(4)):
                c = U_RET + j
                wh, wl = quarter(whi, c % RING), quarter(wlo, c % RING)
                for m in tiles:
                    for kk in ks:
                        k = 4 * j + kk
                        last = products(ps[:, 2 + m, :], xh[:, k, m * P:(m + 1) * P],
                                        xl[:, k, m * P:(m + 1) * P], wh[:, kk, :], wl[:, kk, :],
                                        k == 0, k == KD - 1)
                if m == 1:
                    last.then_inc(used, 1)

            def ret_turn(h, banks):
                for m in range(TT):
                    pe.wait_ge(on_ready, TT * h + m + 1)
                    for j in range(4):
                        last = nc.tensor.transpose(halves(banks[j // 2])[:, j % 2, m * P:(m + 1) * P],
                                                   onrm[:, m, j * P:(j + 1) * P], ident[:])
                last.then_inc(on_turned, 1)

            def ret_head(h):
                for j in range(2, 4):
                    c = U_RET + j
                    unit_ready(pe, c, 2 * h)
                    feature_tile(halves(j - 2)[:, 0, :], c, 0)
                    feature_tile(halves(j - 2)[:, 1, :], c, 1).then_inc(used, 1)
                c = U_RET + 4
                unit_ready(pe, c, 2 * h)
                feature_tile(halves(4)[:, 0, :], c, 0)
                pe.wait_ge(rq_copied, h + 1)
                pe.wait_ge(rk_copied, h + 1)
                for m, (a, b) in enumerate(((0, SEQ), (SEQ, CAUSAL))):
                    for k in range(2):
                        last = nc.tensor.matmul(ps[:, 6, a:b], kT[:, k, m * P:(m + 1) * P],
                                                qT[:, k, m * P:SEQ], start=k == 0, stop=k == 1)
                last.then_inc(rs_ready, 1)
                feature_tile(halves(4)[:, 1, :], c, 1).then_inc(used, 1)
                unit_ready(pe, c + 1, 2 * h)
                feature_tile(halves(5)[:, 0, :], c + 1, 0)
                pe.wait_ge(decayed_lo, h + 1)
                pe.wait_ge(rv_lo, TT * h + TT)
                for bank, a, m, first, last in ((7, 0, 0, True, True), (0, P, 0, True, False),
                                                (0, SEQ, 1, False, True)):
                    ins = products(ps[:, bank, :], sh[:, a:a + P], sl[:, a:a + P], vh[:, m, :], vl[:, m, :],
                                   first, last)
                    if last:
                        ins.then_inc(ro_ready, 1)
                feature_tile(halves(5)[:, 1, :], c + 1, 1).then_inc(used, 1)

            turn_x(0, TR_FFN, 1)
            for j in range(2):
                unit_ready(pe, U_RET + j)
                x_parts(1, 0, j)
                ret_v(0, j, [0], range(2 if j else 4))
            turn_x(1, TR_FFN, 1)
            ret_v(0, 1, [0], range(2, 4))
            for j in range(2):
                x_parts(1, 1, j)
                ret_v(0, j, [1])
            ret_head(0)
            with pe.Fori(1, RH) as h:
                unit_ready(pe, U_RET, 2 * h)
                ret_v(h, 0)
                pe.wait_ge(silu_done, 2 * h)
                ret_turn(h - 1, (4, 5))
                unit_ready(pe, U_RET + 1, 2 * h)
                ret_v(h, 1)
                ret_head(h)

            def ret_out(j, m, kk, columns=range(2)):
                k = 2 * j + kk
                return out_rows(ACC_RET, oh[:, k, :], ol[:, k, :], U_RET_OUT + j, m, kk, k == 0,
                                k == 2 * KD - 1, columns)

            order = [(j, m, kk) for j in range(6) for m in range(TT) for kk in range(2)]
            order += [(j, m, kk) for m in range(TT) for j in range(6, 8) for kk in range(2)]
            for j, m, kk in order[:-2]:
                if (j, m, kk) == (0, 1, 0):
                    pe.wait_ge(silu_done, 2 * RH)
                if (m, kk) == (0, 0):
                    if j == 2:
                        ret_turn(RH - 1, (2, 3))
                    unit_ready(pe, U_RET_OUT + j)
                    pe.wait_ge(ro_lo, j // 2 + 2)
                last = ret_out(j, m, kk)
                if (j, m, kk) == (7, 0, 1):
                    last.then_inc(acc_ready, 1)
                if (m, kk) == (1, 1):
                    last.then_inc(used, 1)
            last_unit(lambda kk, n: ret_out(7, 1, kk, [n]))
            turn_after_ln(2, TR_RET)
            ffn_all(1, 2)


_INS = ["x", "att_w_in", "att_w_out", "ret_w_in", "ret_w_out", "ret_gn_g", "ret_gn_b", "mix_ln_g",
        "mix_ln_b", "ffn_ln_g", "ffn_ln_b", "ffn_w_up", "ffn_conv_w", "ffn_conv_b", "ffn_w_down"]
_OUTS = [((1, SEQ, D), "float32")]


def kernel(**inputs):
    import numpy as _np
    import concourse.bacc as _bacc
    from concourse import mybir as _mybir
    from concourse.bass_utils import run_bass_kernel_spmd as _run

    nc = _bacc.Bacc("TRN2", target_bir_lowering=False, num_devices=1)
    arrays, args = {}, []
    for name in _INS:
        a = _np.ascontiguousarray(inputs[name])
        arrays[f"in_{name}_dram"] = a
        args.append(nc.dram_tensor(f"in_{name}_dram", a.shape, _mybir.dt.from_np(a.dtype), kind="ExternalInput").ap())
    for i, (shape, dtype) in enumerate(_OUTS):
        dt = _mybir.dt.from_np(_np.dtype(dtype))
        args.append(nc.dram_tensor(f"out_{i}_dram", shape, dt, kind="ExternalOutput").ap())
    decoder_trunk(nc, *args)
    r = _run(nc, [arrays], core_ids=[0])
    got = tuple(r.results[0][f"out_{i}_dram"] for i in range(len(_OUTS)))
    return got[0]
```
